# Optimizing a Trainium2 kernel written in Bass

```python
import jax, jax.numpy as jnp
from jax import lax
import numpy as np

D_MODEL = 1024
BATCH = 1
SEQ = 256
DEPTH = 2

CHUNK = 64
HEAD_DIM = 64
N_Q_HEADS = D_MODEL // HEAD_DIM
GQA_GROUP = 8
N_KV_HEADS = N_Q_HEADS // GQA_GROUP
WINDOW = 128
WIN_CHUNKS = WINDOW // CHUNK
ROPE_THETA = 10000.0
CONV_CHANNELS = D_MODEL
CONV_WIDTH = 31
D_FF = 2816
FFN_CONV_WIDTH = 3
EPS = 1e-5
NEG_INF = -1e30

ATTN_W = N_Q_HEADS * HEAD_DIM
KV_W = N_KV_HEADS * HEAD_DIM
IN_PROJ = ATTN_W + 2 * KV_W + 2 * CONV_CHANNELS + 2 * D_MODEL
SPLITS = (ATTN_W, ATTN_W + KV_W, ATTN_W + 2 * KV_W, ATTN_W + 2 * KV_W + 2 * CONV_CHANNELS)

kernel_name = 'hybrid_swa_sink_conformer_conv_convffn'

def rmsnorm(x, g):
    xf = x.astype(jnp.float32)
    y = xf * lax.rsqrt(jnp.mean(xf * xf, axis=-1, keepdims=True) + EPS)
    return (y * g.astype(jnp.float32)).astype(x.dtype)

def layernorm(x, g, b):
    xf = x.astype(jnp.float32)
    mu = jnp.mean(xf, axis=-1, keepdims=True)
    xc = xf - mu
    y = xc * lax.rsqrt(jnp.mean(xc * xc, axis=-1, keepdims=True) + EPS)
    return (y * g.astype(jnp.float32) + b.astype(jnp.float32)).astype(x.dtype)

def rope_tables(positions):
    inv_freq = ROPE_THETA ** (-jnp.arange(0, HEAD_DIM, 2, dtype=jnp.float32) / HEAD_DIM)
    ang = positions.astype(jnp.float32)[..., None] * inv_freq
    return jnp.cos(ang), jnp.sin(ang)

def apply_rope(t, cos, sin):
    tf = t.astype(jnp.float32)
    t1, t2 = jnp.split(tf, 2, axis=-1)
    c = cos[:, :, None, :]
    s = sin[:, :, None, :]
    return jnp.concatenate([t1 * c - t2 * s, t2 * c + t1 * s], axis=-1).astype(t.dtype)

def causal_dwconv(x, w, b):
    k = w.shape[0]
    y = lax.conv_general_dilated(
        x, w[:, None, :].astype(x.dtype), window_strides=(1,), padding=[(k - 1, 0)],
        dimension_numbers=('NWC', 'WIO', 'NWC'), feature_group_count=x.shape[-1])
    return y + b

def _shift_chunks(t, o):
    if o == 0:
        return t
    pad = jnp.zeros_like(t[:, :o])
    return jnp.concatenate([pad, t[:, :-o]], axis=1)

def sliding_window_sink_attention(q, k, v, sinks):
    B, S = q.shape[0], q.shape[1]
    n_chunks = S // CHUNK
    offsets = list(range(WIN_CHUNKS - 1, -1, -1))
    qc = q.reshape(B, n_chunks, CHUNK, N_KV_HEADS, GQA_GROUP, HEAD_DIM)
    kc = k.reshape(B, n_chunks, CHUNK, N_KV_HEADS, HEAD_DIM)
    vc = v.reshape(B, n_chunks, CHUNK, N_KV_HEADS, HEAD_DIM)
    kb = jnp.concatenate([_shift_chunks(kc, o) for o in offsets], axis=2)
    vb = jnp.concatenate([_shift_chunks(vc, o) for o in offsets], axis=2)
    scale = HEAD_DIM ** -0.5
    s = jnp.einsum('bcqkgd,bcjkd->bckgqj', qc, kb).astype(jnp.float32) * scale
    key_chunk_off = jnp.repeat(jnp.array(offsets, dtype=jnp.int32), CHUNK)
    valid = (jnp.arange(n_chunks, dtype=jnp.int32)[:, None] - key_chunk_off[None, :]) >= 0
    s = jnp.where(valid[None, :, None, None, None, :], s, NEG_INF)
    sink = sinks.astype(jnp.float32).reshape(N_KV_HEADS, GQA_GROUP)[None, None, :, :, None, None]
    m = jnp.maximum(jnp.max(s, axis=-1, keepdims=True), sink)
    p = jnp.exp(s - m)
    denom = jnp.sum(p, axis=-1, keepdims=True) + jnp.exp(sink - m)
    probs = (p / denom).astype(v.dtype)
    o = jnp.einsum('bckgqj,bcjkd->bcqkgd', probs, vb)
    return o.reshape(B, S, ATTN_W)

def setup_inputs(seed: int = 0) -> dict:
    key = jax.random.key(seed)
    ks = jax.random.split(key, 20)
    f32 = jnp.float32

    def nrm(k, shape, scale):
        return jax.random.normal(k, shape, f32) * scale

    x = jax.random.normal(ks[0], (BATCH, SEQ, D_MODEL), f32)
    stream_offset = jax.random.randint(ks[1], (BATCH,), 0, 64, dtype=jnp.int32) * CHUNK
    positions = stream_offset[:, None] + jnp.arange(SEQ, dtype=jnp.int32)[None, :]
    return {
        'x': x,
        'positions': positions,
        'attn_norm_g': 1.0 + nrm(ks[2], (DEPTH, D_MODEL), 0.02),
        'w_in': nrm(ks[3], (DEPTH, D_MODEL, IN_PROJ), D_MODEL ** -0.5),
        'attn_sinks': nrm(ks[4], (DEPTH, N_Q_HEADS), 0.5),
        'w_attn_o': nrm(ks[5], (DEPTH, ATTN_W, D_MODEL), ATTN_W ** -0.5),
        'conv_dw_w': nrm(ks[6], (DEPTH, CONV_WIDTH, CONV_CHANNELS), CONV_WIDTH ** -0.5),
        'conv_dw_b': nrm(ks[7], (DEPTH, CONV_CHANNELS), 0.02),
        'conv_ln_g': 1.0 + nrm(ks[8], (DEPTH, CONV_CHANNELS), 0.02),
        'conv_ln_b': nrm(ks[9], (DEPTH, CONV_CHANNELS), 0.02),
        'w_conv_o': nrm(ks[10], (DEPTH, CONV_CHANNELS, D_MODEL), CONV_CHANNELS ** -0.5),
        'w_out': nrm(ks[11], (DEPTH, D_MODEL, D_MODEL), D_MODEL ** -0.5),
        'ffn_norm_g': 1.0 + nrm(ks[12], (DEPTH, D_MODEL), 0.02),
        'w_ffn_up': nrm(ks[13], (DEPTH, D_MODEL, 2 * D_FF), D_MODEL ** -0.5),
        'ffn_dw_w': nrm(ks[14], (DEPTH, FFN_CONV_WIDTH, 2 * D_FF), FFN_CONV_WIDTH ** -0.5),
        'ffn_dw_b': nrm(ks[15], (DEPTH, 2 * D_FF), 0.02),
        'w_ffn_down': nrm(ks[16], (DEPTH, D_FF, D_MODEL), D_FF ** -0.5),
        'final_norm_g': 1.0 + nrm(ks[17], (D_MODEL,), 0.02),
    }

def reference(x, positions, attn_norm_g, w_in, attn_sinks, w_attn_o, conv_dw_w, conv_dw_b,
              conv_ln_g, conv_ln_b, w_conv_o, w_out, ffn_norm_g, w_ffn_up, ffn_dw_w,
              ffn_dw_b, w_ffn_down, final_norm_g):
    B, S = x.shape[0], x.shape[1]
    cos, sin = rope_tables(positions)
    for l in range(DEPTH):
        h = rmsnorm(x, attn_norm_g[l])
        proj = h @ w_in[l]
        q, k, v, conv_in, gate_logits = jnp.split(proj, SPLITS, axis=-1)
        q = apply_rope(q.reshape(B, S, N_Q_HEADS, HEAD_DIM), cos, sin)
        k = apply_rope(k.reshape(B, S, N_KV_HEADS, HEAD_DIM), cos, sin)
        v = v.reshape(B, S, N_KV_HEADS, HEAD_DIM)
        y_attn = sliding_window_sink_attention(q, k, v, attn_sinks[l]) @ w_attn_o[l]
        ca, cb = jnp.split(conv_in, 2, axis=-1)
        u = ca * jax.nn.sigmoid(cb)
        u = causal_dwconv(u, conv_dw_w[l], conv_dw_b[l])
        u = jax.nn.silu(layernorm(u, conv_ln_g[l], conv_ln_b[l]))
        y_conv = u @ w_conv_o[l]
        g_attn, g_conv = jnp.split(gate_logits, 2, axis=-1)
        merged = jax.nn.sigmoid(g_attn) * y_attn + jax.nn.sigmoid(g_conv) * y_conv
        x = x + merged @ w_out[l]
        h = rmsnorm(x, ffn_norm_g[l])
        up = causal_dwconv(h @ w_ffn_up[l], ffn_dw_w[l], ffn_dw_b[l])
        gt, val = jnp.split(up, 2, axis=-1)
        x = x + (jax.nn.silu(gt) * val) @ w_ffn_down[l]
    return rmsnorm(x, final_norm_g)


_drawn_inputs = setup_inputs


def setup_inputs(seed=0):
    import zlib

    import numpy as np

    out = dict(_drawn_inputs(seed))
    spreads = {}
    factors = {'attn_norm_g': 4.548,
     'attn_sinks': 8.0,
     'conv_dw_b': 2.673,
     'conv_ln_g': 4.945,
     'conv_ln_b': 5.633,
     'ffn_norm_g': 2.891,
     'ffn_dw_b': 2.8,
     'final_norm_g': 2.871}
    for name, (base, spread) in spreads.items():
        noise = np.random.default_rng([zlib.crc32(name.encode()), seed]).standard_normal(out[name].shape)
        drawn = base * np.exp(spread * noise) if base else spread * noise
        out[name] = __import__('jax').numpy.asarray(drawn.astype(out[name].dtype))
    for name, factor in factors.items():
        out[name] = (out[name] * factor).astype(out[name].dtype)
    return out
```

```python
import concourse.bass as bass
from concourse import mybir
from contextlib import ExitStack

DEPTH, D_MODEL, SEQ = 2, 1024, 256
CHUNK, HEAD_DIM, N_HEADS, N_KV = 64, 64, 16, 2
CONV_WIDTH, D_FF = 31, 2816
THETA, EPS = 10000.0, 1e-5
P = 128
NT = D_MODEL // P
T = SEQ
FT = D_FF // P
N_CHUNKS = SEQ // CHUNK
N_PAIRS = N_HEADS // 2
GROUPS = N_CHUNKS * N_KV
GROUP_PAIRS = N_PAIRS // N_KV

BLOCKS = 16
UNIT = BLOCKS * P
RING = 3
U_GLU, U_KV, U_Q, U_GATE = 0, 8, 9, 13
U_AO, U_CO, U_OUT, U_FFN = 21, 25, 29, 33
FFN_STEPS = FT // 2
UNITS = U_FFN + 3 * FFN_STEPS
USES = UNITS // RING

PA_G, PA_CB, PA_LG, PA_LB, PA_FG = 0, 8, 16, 24, 32
PA_CW = 40
PA_SINK = PA_CW + NT * CONV_WIDTH
PA_FW = PA_SINK + N_PAIRS
NPAR = PA_FW + 2 * FT * 4
C_FREQ, C_EPS, C_HALFPI, C_SWAP, C_ID = 0, 1, 2, 4, 132
NCONST = 260

CONV_STEPS = CONV_WIDTH * NT // 2
ROUNDING = 1.5 * 2.0 ** 23
PI_BELOW = 3.1415925
ANGLE_SCALES = (2 ** 20, 2 ** 10, 1)
TABLE_STEPS = 4 + 5 * len(ANGLE_SCALES)


def pi_parts(scale):
    import numpy as np
    rest, parts = np.float64(2 * np.pi * scale), []
    for _ in range(2):
        unit = 2.0 ** (np.floor(np.log2(rest)) - 11)
        parts.append(float(np.floor(rest / unit) * unit))
        rest = rest - parts[-1]
    return parts + [float(np.float32(rest))]


def hybrid_encoder(nc, x_in, pos_in, const_in, par_in, gf_in, w_in, y_out):
    f32, f32r, i32 = mybir.dt.float32, mybir.dt.float32r, mybir.dt.int32
    ALU, ACT, AX = mybir.AluOpType, mybir.ActivationFunctionType, mybir.AxisListType
    ctx = ExitStack()
    with ctx:
        def sb(name, shape, dt=f32):
            return ctx.enter_context(nc.sbuf_tensor(name, shape, dt))

        def pb(name):
            return ctx.enter_context(nc.psum_tensor(name, [P, 2, T], f32))

        def sem(name):
            return ctx.enter_context(nc.semaphore(name))

        raw = [sb(f"raw{s}", [P, UNIT]) for s in range(RING)]
        whi = [sb(f"whi{s}", [P, UNIT], f32r) for s in range(RING)]
        wlo = [sb(f"wlo{s}", [P, UNIT], f32r) for s in range(RING)]
        x = sb("x", [P, NT, T])
        hh, hl = sb("hh", [P, NT, T], f32r), sb("hl", [P, NT, T], f32r)
        oh, ol = sb("oh", [P, NT, T], f32r), sb("ol", [P, NT, T], f32r)
        uh, ul = sb("uh", [P, NT, T], f32r), sb("ul", [P, NT, T], f32r)
        fh, fl = oh[:, 0:4, :], ol[:, 0:4, :]
        const = sb("const", [P, NCONST])
        ones = sb("ones", [P, P])
        par_all = sb("par_all", [P, DEPTH * NPAR])
        par = sb("par", [P, NPAR])
        gf = sb("gf", [P, NT])
        cos, sin = sb("cos", [P, T]), sb("sin", [P, T])
        upad = sb("upad", [P, NT, CONV_WIDTH - 1 + T])
        cv = sb("cv", [P, NT, T])
        gate = sb("gate", [P, 2, NT, T])
        qk = sb("qk", [P, 4096])
        qr = qk[0:HEAD_DIM, :].rearrange("p (i c o t) -> p i c o t", i=N_PAIRS, c=N_CHUNKS, o=2)
        sq = qk[:, 0:2048].rearrange("p (n t) -> p n t", n=NT)
        h32 = qk[:, 2048:4096].rearrange("p (n t) -> p n t", n=NT)
        fbuf = qk[:, 2048:4096].rearrange("p (a n t) -> p a n t", a=2, n=4)
        kvraw = sb("kvraw", [P, 2, T])
        kr = sb("kr", [HEAD_DIM, N_KV, T])
        vwin = sb("vwin", [P, N_CHUNKS, P])
        probs = [sb(f"probs{i}", [P, GROUP_PAIRS, P]) for i in range(2)]
        probsT = [sb(f"probsT{i}", [P, GROUP_PAIRS, P]) for i in range(2)]
        small = sb("small", [P, 2, 8, GROUP_PAIRS])
        sink8 = sb("sink8", [P, N_PAIRS])
        rstd, lnv = sb("rstd", [P, T]), sb("lnv", [P, T])
        qraw = [gate[:, 0, 4 + 2 * i:6 + 2 * i, :] for i in range(2)]
        rope_a, rope_b = gate[:, 1, 4:6, :], gate[:, 1, 6:8, :]

        pos_i = probs[0][:, 0:2, :].bitcast(i32)
        ang, turns = probsT[0][:, 0:2, :], probsT[0][:, 2:4, :]
        aabs = probsT[1][:, 0:2, :]

        pu = [pb(f"pu{s}") for s in range(RING)]
        ps = [pb(f"ps{i}") for i in range(2)]
        pt, po, pc = pb("pt"), pb("po"), pb("pc")
        down = [ps[0], ps[1], pt, pc]

        raw_in = [sem(f"raw_in{s}") for s in range(RING)]
        hi_ready = [sem(f"hi_ready{s}") for s in range(RING)]
        lo_ready = [sem(f"lo_ready{s}") for s in range(RING)]
        unit_done = [sem(f"unit_done{s}") for s in range(RING)]
        x_in_s, c_in, pos_s, par_in_s = sem("x_in"), sem("const_in"), sem("pos_in"), sem("par_in")
        setup, table, act_table = sem("setup"), sem("table"), sem("act_table")
        par_ready, pad_zero = sem("par_ready"), sem("pad_zero")
        sq_ready, stat_done, ln_done, rstd_ready = sem("sq_ready"), sem("stat_done"), sem("ln_done"), sem("rstd_ready")
        h32_ready, hh_ready, hl_ready, x_ready = sem("h32_ready"), sem("hh_ready"), sem("hl_ready"), sem("x_ready")
        glu_tanh, u_ready, conv_step = sem("glu_tanh"), sem("u_ready"), sem("conv_step")
        kv_raw, q_raw, rot_done, rope_ab, rope_done = sem("kv_raw"), sem("q_raw"), sem("rot_done"), sem("rope_ab"), sem("rope_done")
        vt_done, v_ready = sem("vt_done"), sem("v_ready")
        s_done, mx_step, exp_done, den_step, p_ready = sem("s_done"), sem("mx_step"), sem("exp_done"), sem("den_step"), sem("p_ready")
        tr_done, pt_ready, pv_done, oh_ready, ol_ready = sem("tr_done"), sem("pt_ready"), sem("pv_done"), sem("oh_ready"), sem("ol_ready")
        xc_ready, t_ready, silu_ready, uh_ready, ul_ready = sem("xc_ready"), sem("t_ready"), sem("silu_ready"), sem("uh_ready"), sem("ul_ready")
        gate_ready, m_step = sem("gate_ready"), sem("m_step")
        down_zero, f_conv0, f_tap, f_silu, f_ready, fh_ready, fl_ready = [
            sem(n) for n in ("down_zero", "f_conv0", "f_tap", "f_silu", "f_ready", "fh_ready", "fl_ready")]
        y_ready, y_out_s = sem("y_ready"), sem("y_out")

        def uses(l, u):
            return l * USES + u // RING

        def result_read(l, u):
            if u < U_KV:
                return u_ready, l * NT + u + 1
            if u < U_Q:
                return kv_raw, l + 1
            if u < U_GATE:
                return q_raw, l * 4 + u - U_Q + 1
            if u < U_AO:
                return gate_ready, l * NT + u - U_GATE + 1
            if u < U_CO:
                return m_step, l * 12 + u - U_AO + 1
            if u < U_OUT:
                return m_step, l * 12 + 4 + 2 * (u - U_CO) + 1
            return x_ready, l * 8 + u - U_OUT + 1

        block = ctx.enter_context(nc.Block())

        @block.sync
        def _(sp):
            sp.dma_start(x[:, :, :], x_in).then_inc(x_in_s, 16)
            sp.dma_start(const[:, :], const_in).then_inc(c_in, 16)
            def load_unit(s, at):
                sp.dma_start(raw[s][:, :], w_in[at, :, :].rearrange("a p n -> p (a n)")).then_inc(raw_in[s], 16)

            for s in range(RING):
                load_unit(s, slice(s, s + 1))
            with sp.Fori(1, DEPTH * USES) as r:
                for s in range(RING):
                    sp.wait_ge(lo_ready[s], r)
                    load_unit(s, bass.ds(r * RING + s, 1))
            for half in range(2):
                sp.wait_ge(y_ready, NT // 2 * (half + 1))
                sp.dma_start(y_out[:, 4 * half:4 * half + 4, :], h32[:, 4 * half:4 * half + 4, :]).then_inc(y_out_s, 16)
            sp.wait_ge(y_out_s, 32)

        @block.gpsimd
        def _(pool):
            nc.gpsimd.memset(ones[:, :], 1.0 / D_MODEL).then_inc(setup, 1)
            nc.gpsimd.memset(upad[:, :, 0:CONV_WIDTH - 1], 0.0).then_inc(pad_zero, 1)
            def split_low(s, n):
                pool.wait_ge(hi_ready[s], n + 1)
                nc.gpsimd.tensor_tensor(wlo[s][:, :], raw[s][:, :], whi[s][:, :].bitcast(f32), ALU.subtract).then_inc(lo_ready[s], 1)

            with pool.Fori(0, DEPTH) as l:
                with pool.Fori(0, U_FFN // RING) as r:
                    for s in range(RING):
                        split_low(s, l * USES + r)
                with pool.Fori(12, USES) as n:
                    split_low(1, l * USES + n)

        @block.scalar
        def _(act):
            A = nc.scalar.activation
            act.dma_start(pos_i, pos_in.partition_broadcast(P)).then_inc(pos_s, 16)
            act.dma_start(par_all[:, :], par_in).then_inc(par_in_s, 16)
            act.dma_start(gf[:, :], gf_in).then_inc(par_in_s, 16)

            def split_high(l, s, n):
                act.wait_ge(raw_in[s], (l * USES + n + 1) * 16)
                act.wait_ge(unit_done[s], l * USES + n + 1)
                A(whi[s][:, :], raw[s][:, :], ACT.Copy).then_inc(hi_ready[s], 1)

            def next_high(l, u):
                if u + RING < UNITS:
                    split_high(l, (u + RING) % RING, (u + RING) // RING)

            def inverse_root(bank, stats, roots):
                act.wait_ge(stat_done, stats)
                A(lnv[:, :], bank, ACT.Ln, bias=const[:, C_EPS:C_EPS + 1]).then_inc(ln_done, 1)
                act.wait_ge(ln_done, roots)
                A(rstd[:, :], lnv[:, :], ACT.Exp, scale=-0.5).then_inc(rstd_ready, 1)

            def high_of_h(before):
                for p in range(NT // 2):
                    act.wait_ge(h32_ready, before + 2 * p + 2)
                    A(hh[:, 2 * p:2 * p + 2, :], h32[:, 2 * p:2 * p + 2, :], ACT.Copy).then_inc(hh_ready, 1)

            act.wait_ge(x_in_s, 16)
            for p in range(NT // 2):
                A(sq[:, 2 * p:2 * p + 2, :], x[:, 2 * p:2 * p + 2, :], ACT.Square).then_inc(sq_ready, 1)
            act.wait_ge(c_in, 16)
            inverse_root(po[:, 0, :], 1, 1)
            act.wait_ge(table, TABLE_STEPS)
            A(sin[:, :], ang, ACT.Sin).then_inc(act_table, 1)
            A(cos[:, :], aabs, ACT.Sin, scale=-1.0, bias=const[:, C_HALFPI:C_HALFPI + 1]).then_inc(act_table, 1)

            with act.Fori(0, DEPTH) as l:
                split_high(l, 0, 0)
                high_of_h(l * 2 * NT)
                split_high(l, 1, 0)
                split_high(l, 2, 0)
                for i in range(NT):
                    u = U_GLU + i
                    act.wait_ge(unit_done[u % RING], uses(l, u) + 2)
                    if i >= 2:
                        act.wait_ge(u_ready, l * NT + i - 1)
                    A(kvraw[:, i % 2, :], pu[u % RING][:, 1, :], ACT.Tanh, scale=0.5).then_inc(glu_tanh, 1)
                    next_high(l, u)
                u = U_KV
                act.wait_ge(unit_done[u % RING], uses(l, u) + 2)
                act.wait_ge(u_ready, l * NT + NT)
                A(kvraw[:, :, :], pu[u % RING][:, :, :], ACT.Copy).then_inc(kv_raw, 1)
                next_high(l, u)
                for i in range(4):
                    u = U_Q + i
                    act.wait_ge(unit_done[u % RING], uses(l, u) + 2)
                    if i >= 2:
                        act.wait_ge(rope_done, l * 10 + 2 * i)
                    A(qraw[i % 2], pu[u % RING][:, :, :], ACT.Copy).then_inc(q_raw, 1)
                    if i == 1:
                        act.wait_ge(vt_done, l + 1)
                        A(vwin[0:CHUNK, 0, :], po[0:CHUNK, 0, 0:P], ACT.Copy).then_inc(v_ready, 1)
                        A(vwin[:, 1:N_CHUNKS, :], po[:, :, :].rearrange("p a (b t) -> p (a b) t", t=P)[:, 1:N_CHUNKS, :], ACT.Copy).then_inc(v_ready, 1)
                    next_high(l, u)

                def evict_transposed(n):
                    act.wait_ge(tr_done, l * GROUPS + n + 1)
                    A(probsT[n % 2][:, :, :], pt[:, :, :].rearrange("p a (b t) -> p (a b) t", t=P), ACT.Copy).then_inc(pt_ready, 1)

                def high_of_o(n):
                    c, g = n % N_CHUNKS, n // N_CHUNKS
                    act.wait_ge(pv_done, l * GROUPS + n + 1)
                    src = po[0:HEAD_DIM, :, :].rearrange("p a (b h t) -> p (a b) h t", b=2, h=2)
                    for odd in range(2):
                        A(oh[64 * odd:64 * odd + 64, 4 * g:4 * g + 4, CHUNK * c:CHUNK * c + CHUNK], src[:, :, odd, :], ACT.Copy).then_inc(oh_ready, 1)

                def exps(n):
                    keys = CHUNK if n % N_CHUNKS == 0 else P
                    g = n // N_CHUNKS
                    act.wait_ge(mx_step, (l * GROUPS + n) * 4 + 4)
                    scores = ps[n % 2][:, :, :].rearrange("p a (b t) -> p (a b) t", t=P)
                    sm = small[:, n % 2, :, :]
                    A(sm[:, 4, :], sm[:, 3, :], ACT.Exp)
                    for j in range(GROUP_PAIRS):
                        last = A(probs[n % 2][:, j, 0:keys], scores[:, j, 0:keys], ACT.Exp, scale=HEAD_DIM ** -0.5,
                                 bias=sm[:, 2, j:j + 1], accum_out=sm[:, 5, j:j + 1])
                    last.then_inc(exp_done, 1)

                for i in range(NT):
                    u = U_GATE + i
                    if i >= 1:
                        evict_transposed(i - 1)
                    exps(i)
                    if i >= 2:
                        high_of_o(i - 2)
                    if i == 4:
                        act.wait_ge(rope_done, l * 10 + 10)
                    act.wait_ge(unit_done[u % RING], uses(l, u) + 2)
                    A(gate[:, :, i, :], pu[u % RING][:, :, :], ACT.Tanh, scale=0.5).then_inc(gate_ready, 1)
                    next_high(l, u)
                evict_transposed(GROUPS - 1)
                high_of_o(GROUPS - 2)
                high_of_o(GROUPS - 1)
                next_high(l, U_AO)
                next_high(l, U_AO + 1)
                for p in range(NT // 2):
                    act.wait_ge(xc_ready, l * 4 + p + 1)
                    A(sq[:, 2 * p:2 * p + 2, :], cv[:, 2 * p:2 * p + 2, :], ACT.Square).then_inc(sq_ready, 1)
                next_high(l, U_AO + 2)
                inverse_root(ps[0][:, 0, :], l * 4 + 3, l * 3 + 2)
                for p in range(NT // 2):
                    act.wait_ge(t_ready, l * 4 + p + 1)
                    for t in (2 * p, 2 * p + 1):
                        last = A(cv[:, t, :], cv[:, t, :], ACT.Silu, scale=par[:, PA_LG + t:PA_LG + t + 1],
                                 bias=par[:, PA_LB + t:PA_LB + t + 1])
                    last.then_inc(silu_ready, 1)
                    act.wait_ge(silu_ready, l * 4 + p + 1)
                    A(uh[:, 2 * p:2 * p + 2, :], cv[:, 2 * p:2 * p + 2, :], ACT.Copy).then_inc(uh_ready, 1)
                next_high(l, U_AO + 3)
                for i in range(4):
                    act.wait_ge(m_step, l * 12 + 4 + 2 * i + 2)
                    A(hh[:, 2 * i:2 * i + 2, :], gate[:, 1, 2 * i:2 * i + 2, :], ACT.Copy, scale=0.5).then_inc(hh_ready, 1)
                    next_high(l, U_CO + i)
                for i in range(4):
                    act.wait_ge(x_ready, l * 8 + i + 1)
                    A(sq[:, 2 * i:2 * i + 2, :], x[:, 2 * i:2 * i + 2, :], ACT.Square).then_inc(sq_ready, 1)
                    next_high(l, U_OUT + i)
                inverse_root(po[:, 0, :], l * 4 + 4, l * 3 + 3)
                high_of_h(l * 2 * NT + NT)

                def hidden_tile(k, ab, bank, done_sem, done_value, gcol, vcol, before=None):
                    act.wait_ge(done_sem, done_value)
                    if before is not None:
                        act.wait_ge(f_ready, before)
                    for half, col in ((0, gcol), (1, vcol)):
                        A(fbuf[:, ab, half, :], bank[:, half, :], ACT.Identity, scale=par[:, bass.ds(col + 2, 1)],
                          bias=par[:, bass.ds(col + 3, 1)]).then_inc(f_conv0, 1)
                    act.wait_ge(f_tap, k * 4 + 3)
                    A(fbuf[:, ab, 2, :], fbuf[:, ab, 0, :], ACT.Silu).then_inc(f_silu, 1)

                def hidden_high(k, ab, parity):
                    act.wait_ge(f_ready, k + 1)
                    A(fh[:, 2 * parity + ab, :], fbuf[:, ab, 3, :], ACT.Copy).then_inc(fh_ready, 1)

                base = l * FT
                hidden_tile(base, 0, pu[0], unit_done[0], uses(l, U_FFN) + 2, PA_FW, PA_FW + FT * 4)
                next_high(l, U_FFN)
                hidden_high(base, 0, 0)
                hidden_tile(base + 1, 1, pu[1], unit_done[1], uses(l, U_FFN + 1) + 2, PA_FW + 4, PA_FW + FT * 4 + 4)
                next_high(l, U_FFN + 1)
                hidden_high(base + 1, 1, 0)

                def ffn_step(j, parity, last):
                    k = j * 2 + l * FT
                    col = j * 8 + PA_FW
                    hidden_tile(k, 0, pu[2], unit_done[2], l * USES + j + 12, col, col + FT * 4, k - 1)
                    split_high(l, 2, j + 11)
                    act.wait_ge(unit_done[1], l * USES + j + 12)
                    hidden_high(k, 0, parity)
                    hidden_tile(k + 1, 1, pu[0], unit_done[0], l * USES + j + 13, col + 4, col + FT * 4 + 4, k)
                    if not last:
                        split_high(l, 0, j + 12)
                    hidden_high(k + 1, 1, parity)
                    if not last:
                        split_high(l, 1, j + 12)

                with act.Fori(0, FFN_STEPS // 2 - 1) as r:
                    ffn_step(r * 2 + 1, 1, False)
                    ffn_step(r * 2 + 2, 0, False)
                ffn_step(FFN_STEPS - 2, 1, False)
                ffn_step(FFN_STEPS - 1, 0, True)
                for i in range(4):
                    act.wait_ge(x_ready, l * 8 + 4 + i + 1)
                    A(sq[:, 2 * i:2 * i + 2, :], x[:, 2 * i:2 * i + 2, :], ACT.Square).then_inc(sq_ready, 1)
                inverse_root(po[:, 0, :], l * 4 + 5, l * 3 + 4)

        @block.vector
        def _(dve):
            V = nc.vector
            V.memset(vwin[CHUNK:P, 0, :], 0.0).then_inc(setup, 1)
            done = [0]

            def step(instruction):
                done[0] += 1
                instruction.then_inc(table, 1)
                dve.wait_ge(table, done[0])

            dve.wait_ge(pos_s, 16)
            dve.wait_ge(c_in, 16)
            step(V.tensor_copy(ang, pos_i))
            step(V.tensor_scalar(ang, ang, const[:, C_FREQ:C_FREQ + 1], None, ALU.mult))
            for scale in ANGLE_SCALES:
                parts = pi_parts(scale)
                step(V.tensor_scalar(turns, ang, 1.0 / sum(parts), ROUNDING, ALU.mult, ALU.add))
                step(V.tensor_scalar(turns, turns, -ROUNDING, None, ALU.add))
                for part in parts:
                    step(V.scalar_tensor_tensor(ang, turns, -part, ang, ALU.mult, ALU.add))
            step(V.tensor_scalar(ang, ang, PI_BELOW, -PI_BELOW, ALU.min, ALU.max))
            step(V.scalar_tensor_tensor(aabs, ang, -1.0, ang, ALU.mult, ALU.max))
            assert done[0] == TABLE_STEPS
            dve.wait_ge(par_in_s, 32)

            def normalise(l, gain, before, roots, hh_before):
                dve.wait_ge(rstd_ready, roots)

                def low(p):
                    dve.wait_ge(hh_ready, hh_before + p + 1)
                    V.tensor_tensor(hl[:, 2 * p:2 * p + 2, :], h32[:, 2 * p:2 * p + 2, :],
                                    hh[:, 2 * p:2 * p + 2, :].bitcast(f32), ALU.subtract).then_inc(hl_ready, 1)

                for p in range(NT // 2):
                    for t in (2 * p, 2 * p + 1):
                        V.scalar_tensor_tensor(h32[:, t, :], x[:, t, :], gain[:, t:t + 1], rstd[:, :],
                                               ALU.mult, ALU.mult).then_inc(h32_ready, 1)
                    if p:
                        low(p - 1)
                low(NT // 2 - 1)

            with dve.Fori(0, DEPTH) as l:
                V.tensor_copy(par[:, :], par_all[:, bass.ds(l * NPAR, NPAR)]).then_inc(par_ready, 1)
                dve.wait_ge(par_ready, l * 3 + 1)
                V.tensor_scalar(par[:, PA_CW:PA_CW + NT * CONV_WIDTH], par[:, PA_CW:PA_CW + NT * CONV_WIDTH], 0.5, None, ALU.mult).then_inc(par_ready, 1)
                V.tensor_scalar(sink8[:, :], par[:, PA_SINK:PA_SINK + N_PAIRS], float(HEAD_DIM) ** 0.5, None, ALU.mult).then_inc(par_ready, 1)
                normalise(l, par[:, PA_G:PA_G + NT], l * 2 * NT, l * 3 + 1, l * 12)
                dve.wait_ge(pad_zero, 1)
                dve.wait_ge(par_ready, l * 3 + 3)

                def glu(i):
                    u = U_GLU + i
                    dve.wait_ge(glu_tanh, l * NT + i + 1)
                    V.scalar_tensor_tensor(upad[:, i, CONV_WIDTH - 1:], kvraw[:, i % 2, :], 1.0, pu[u % RING][:, 0, :],
                                           ALU.add, ALU.mult).then_inc(u_ready, 1)

                def conv(first, last):
                    for n in range(first, last):
                        pair, k = n // CONV_WIDTH, n % CONV_WIDTH
                        if k == 0:
                            dve.wait_ge(u_ready, l * NT + 2 * pair + 2)
                        for j in range(2):
                            t = 2 * pair + j
                            w = par[:, PA_CW + t * CONV_WIDTH + k:PA_CW + t * CONV_WIDTH + k + 1]
                            if n:
                                dve.wait_ge(conv_step, l * 2 * CONV_STEPS + 2 * n + j - 1)
                            if k == 0:
                                V.tensor_scalar(pc[:, j, :], upad[:, t, 0:T], w, par[:, PA_CB + t:PA_CB + t + 1],
                                                ALU.mult, ALU.add).then_inc(conv_step, 1)
                            else:
                                out = cv[:, t, :] if k == CONV_WIDTH - 1 else pc[:, j, :]
                                V.scalar_tensor_tensor(out, upad[:, t, k:k + T], w, pc[:, j, :],
                                                       ALU.mult, ALU.add).then_inc(conv_step, 1)

                glu(0)
                for i in range(1, NT):
                    glu(i)
                    conv(6 * (i - 1), 6 * i)

                def rotate(n, src, tiles, outs):
                    a, b = rope_a[:, 0:tiles, :], rope_b[:, 0:tiles, :]
                    c = cos[:, :].unsqueeze(1).to_broadcast([P, tiles, T])
                    s = sin[:, :].unsqueeze(1).to_broadcast([P, tiles, T])
                    if n:
                        dve.wait_ge(rope_done, l * 10 + 2 * n)
                    V.tensor_tensor(a, src, c, ALU.mult).then_inc(rope_ab, 1)
                    dve.wait_ge(rot_done, l * 5 + n + 1)
                    V.tensor_tensor(b, pt[:, 0:tiles, :], s, ALU.mult).then_inc(rope_ab, 1)
                    dve.wait_ge(rope_ab, l * 10 + 2 * n + 2)
                    for odd in range(2):
                        rows = slice(64 * odd, 64 * odd + 64)
                        split = [v[rows].rearrange("p n (c t) -> p n c t", c=N_CHUNKS) for v in (a, b)]
                        V.tensor_tensor(outs[odd], split[0], split[1], ALU.add).then_inc(rope_done, 1)

                dve.wait_ge(act_table, 2)
                dve.wait_ge(kv_raw, l + 1)
                rotate(0, kvraw[:, 0:1, :], 1, [kr[:, g:g + 1, :].rearrange("p n (c t) -> p n c t", c=N_CHUNKS) for g in range(N_KV)])
                conv(42, 46)
                for i in range(4):
                    dve.wait_ge(q_raw, l * 4 + i + 1)
                    rotate(1 + i, qraw[i % 2], 2, [qr[:, 2 * i:2 * i + 2, :, odd, :] for odd in range(2)])
                    conv(46 + 4 * i, 50 + 4 * i)

                def maxima(n):
                    g = n // N_CHUNKS
                    keys = CHUNK if n % N_CHUNKS == 0 else P
                    scores = ps[n % 2][:, :, :].rearrange("p a (b t) -> p (a b) t", t=P)[:, :, 0:keys]
                    sm = small[:, n % 2, :, :]
                    first = (l * GROUPS + n) * 4
                    dve.wait_ge(s_done, l * GROUPS + n + 1)
                    V.tensor_reduce(sm[:, 0, :], scores, AX.X, ALU.max).then_inc(mx_step, 1)
                    dve.wait_ge(mx_step, first + 1)
                    V.tensor_tensor(sm[:, 1, :], sm[:, 0, :], sink8[:, 4 * g:4 * g + 4], ALU.max).then_inc(mx_step, 1)
                    dve.wait_ge(mx_step, first + 2)
                    V.tensor_scalar(sm[:, 2, :], sm[:, 1, :], -(HEAD_DIM ** -0.5), None, ALU.mult).then_inc(mx_step, 1)
                    dve.wait_ge(mx_step, first + 3)
                    V.tensor_tensor(sm[:, 3, :], sm[:, 2, :], par[:, PA_SINK + 4 * g:PA_SINK + 4 * g + 4], ALU.add).then_inc(mx_step, 1)

                def probabilities(n):
                    keys = CHUNK if n % N_CHUNKS == 0 else P
                    sm = small[:, n % 2, :, :]
                    first = (l * GROUPS + n) * 2
                    dve.wait_ge(exp_done, l * GROUPS + n + 1)
                    V.tensor_tensor(sm[:, 6, :], sm[:, 5, :], sm[:, 4, :], ALU.add).then_inc(den_step, 1)
                    dve.wait_ge(den_step, first + 1)
                    V.reciprocal(sm[:, 7, :], sm[:, 6, :]).then_inc(den_step, 1)
                    dve.wait_ge(den_step, first + 2)
                    if keys < P:
                        V.memset(probs[n % 2][:, :, keys:P], 0.0)
                    pr = probs[n % 2][:, :, 0:keys]
                    V.tensor_tensor(pr, pr, sm[:, 7, :].unsqueeze(2).to_broadcast([P, GROUP_PAIRS, keys]), ALU.mult).then_inc(p_ready, 1)

                def low_of_o(n):
                    c, g = n % N_CHUNKS, n // N_CHUNKS
                    src = po[0:HEAD_DIM, :, :].rearrange("p a (b h t) -> p (a b) h t", b=2, h=2)
                    dve.wait_ge(oh_ready, (l * GROUPS + n) * 2 + 2)
                    for odd in range(2):
                        at = (slice(64 * odd, 64 * odd + 64), slice(4 * g, 4 * g + 4), slice(CHUNK * c, CHUNK * c + CHUNK))
                        last = V.tensor_tensor(ol[at], src[:, :, odd, :], oh[at].bitcast(f32), ALU.subtract)
                    last.then_inc(ol_ready, 1)

                for i in range(GROUPS):
                    maxima(i)
                    conv(62 + 6 * i, 65 + 6 * i)
                    probabilities(i)
                    conv(65 + 6 * i, 68 + 6 * i)
                    if i >= 2:
                        low_of_o(i - 2)
                low_of_o(GROUPS - 2)
                low_of_o(GROUPS - 1)

                def merge_attention(i):
                    u = U_AO + i
                    dve.wait_ge(gate_ready, l * NT + NT)
                    dve.wait_ge(unit_done[u % RING], uses(l, u) + 2)
                    g0 = gate[:, 0, 2 * i:2 * i + 2, :]
                    V.scalar_tensor_tensor(g0, g0, 1.0, pu[u % RING][:, :, :], ALU.add, ALU.mult).then_inc(m_step, 1)

                conv(110, 117)
                merge_attention(0)
                conv(117, CONV_STEPS)
                merge_attention(1)
                dve.wait_ge(stat_done, l * 4 + 2)
                for p in range(NT // 2):
                    c2 = cv[:, 2 * p:2 * p + 2, :]
                    V.tensor_tensor(c2, c2, pt[:, 0, :].unsqueeze(1).to_broadcast([P, 2, T]), ALU.subtract).then_inc(xc_ready, 1)
                merge_attention(2)
                merge_attention(3)
                dve.wait_ge(rstd_ready, l * 3 + 2)
                for p in range(NT // 2):
                    c2 = cv[:, 2 * p:2 * p + 2, :]
                    dve.wait_ge(xc_ready, l * 4 + p + 1)
                    V.tensor_tensor(c2, c2, rstd[:, :].unsqueeze(1).to_broadcast([P, 2, T]), ALU.mult).then_inc(t_ready, 1)
                for p in range(NT // 2):
                    dve.wait_ge(uh_ready, l * 4 + p + 1)
                    V.tensor_tensor(ul[:, 2 * p:2 * p + 2, :], cv[:, 2 * p:2 * p + 2, :], uh[:, 2 * p:2 * p + 2, :].bitcast(f32),
                                    ALU.subtract).then_inc(ul_ready, 1)
                for bank in down:
                    last = V.memset(bank[:, :, :], 0.0)
                last.then_inc(down_zero, 1)
                for i in range(4):
                    u = U_CO + i
                    dve.wait_ge(unit_done[u % RING], uses(l, u) + 2)
                    dve.wait_ge(m_step, l * 12 + 4 + 2 * i)
                    g1 = gate[:, 1, 2 * i:2 * i + 2, :]
                    V.scalar_tensor_tensor(g1, g1, 1.0, pu[u % RING][:, :, :], ALU.add, ALU.mult).then_inc(m_step, 1)
                    dve.wait_ge(m_step, l * 12 + 4 + 2 * i + 1)
                    V.tensor_tensor(g1, g1, gate[:, 0, 2 * i:2 * i + 2, :], ALU.add).then_inc(m_step, 1)
                    dve.wait_ge(hh_ready, l * 12 + 4 + i + 1)
                    V.scalar_tensor_tensor(hl[:, 2 * i:2 * i + 2, :], g1, 0.5, hh[:, 2 * i:2 * i + 2, :].bitcast(f32),
                                           ALU.mult, ALU.subtract).then_inc(hl_ready, 1)
                for i in range(4):
                    u = U_OUT + i
                    dve.wait_ge(unit_done[u % RING], uses(l, u) + 2)
                    x2 = x[:, 2 * i:2 * i + 2, :]
                    V.tensor_tensor(x2, pu[u % RING][:, :, :], x2, ALU.add).then_inc(x_ready, 1)
                for s in range(2):
                    dve.wait_ge(hi_ready[s], l * USES + 12)
                    V.tensor_tensor(wlo[s][:, :], raw[s][:, :], whi[s][:, :].bitcast(f32), ALU.subtract).then_inc(lo_ready[s], 1)
                normalise(l, par[:, PA_FG:PA_FG + NT], l * 2 * NT + NT, l * 3 + 3, l * 12 + 8)

                def hidden_tile(k, ab, s, gcol, vcol):
                    for m in range(4):
                        half, tap = m % 2, 1 - m // 2
                        shift = 2 - tap
                        if m < 2:
                            dve.wait_ge(f_conv0, k * 2 + 2)
                        else:
                            dve.wait_ge(f_tap, k * 4 + m - 1)
                        col = (gcol, vcol)[half] + tap
                        acc = fbuf[:, ab, half, shift:T]
                        last = V.scalar_tensor_tensor(acc, pu[s][:, half, 0:T - shift], par[:, bass.ds(col, 1)], acc,
                                                      ALU.mult, ALU.add).then_inc(f_tap, 1)
                    dve.wait_ge(f_tap, k * 4 + 4)
                    dve.wait_ge(f_silu, k + 1)
                    V.tensor_tensor(fbuf[:, ab, 3, :], fbuf[:, ab, 2, :], fbuf[:, ab, 1, :], ALU.mult).then_inc(f_ready, 1)

                def hidden_low(k, ab, parity):
                    dve.wait_ge(fh_ready, k + 1)
                    V.tensor_tensor(fl[:, 2 * parity + ab, :], fbuf[:, ab, 3, :], fh[:, 2 * parity + ab, :].bitcast(f32), ALU.subtract).then_inc(fl_ready, 1)

                def split_low(s, n):
                    dve.wait_ge(hi_ready[s], l * USES + n + 1)
                    V.tensor_tensor(wlo[s][:, :], raw[s][:, :], whi[s][:, :].bitcast(f32), ALU.subtract).then_inc(lo_ready[s], 1)

                k0 = l * FT
                split_low(2, 11)
                hidden_tile(k0, 0, 0, PA_FW, PA_FW + FT * 4)
                split_low(0, 12)
                hidden_low(k0, 0, 0)
                hidden_tile(k0 + 1, 1, 1, PA_FW + 4, PA_FW + FT * 4 + 4)
                hidden_low(k0 + 1, 1, 0)

                def ffn_step(j, parity, last):
                    k = j * 2 + l * FT
                    col = j * 8 + PA_FW
                    hidden_tile(k, 0, 2, col, col + FT * 4)
                    split_low(2, j + 11)
                    hidden_low(k, 0, parity)
                    hidden_tile(k + 1, 1, 0, col + 4, col + FT * 4 + 4)
                    if not last:
                        split_low(0, j + 12)
                    hidden_low(k + 1, 1, parity)

                with dve.Fori(0, FFN_STEPS // 2 - 1) as r:
                    ffn_step(r * 2 + 1, 1, False)
                    ffn_step(r * 2 + 2, 0, False)
                ffn_step(FFN_STEPS - 2, 1, False)
                ffn_step(FFN_STEPS - 1, 0, True)
                dve.wait_ge(unit_done[2], l * USES + USES + 1)
                for i in range(4):
                    x2 = x[:, 2 * i:2 * i + 2, :]
                    V.tensor_tensor(x2, down[i][:, :, :], x2, ALU.add).then_inc(x_ready, 1)

            dve.wait_ge(rstd_ready, DEPTH * 3 + 1)
            for t in range(NT):
                V.scalar_tensor_tensor(h32[:, t, :], x[:, t, :], gf[:, t:t + 1], rstd[:, :], ALU.mult, ALU.mult).then_inc(y_ready, 1)

        @block.tensor
        def _(pe):
            MM = nc.tensor.matmul

            def product(out, s, block, hi, lo, start, stop, accumulate=False):
                w = slice(block * P, block * P + P)
                MM(out, whi[s][:, w], hi, start=start, stop=False, skip_group_check=accumulate)
                MM(out, whi[s][:, w], lo, start=False, stop=False, skip_group_check=accumulate)
                return MM(out, wlo[s][:, w], hi, start=False, stop=stop, skip_group_check=accumulate)

            def unit(s, uses_before, hi, lo, ready=None):
                pe.wait_ge(hi_ready[s], uses_before + 1)
                pe.wait_ge(lo_ready[s], uses_before + 1)
                for m in range(2):
                    for k in range(NT):
                        if ready is not None and m == 0 and k % 2 == 0:
                            ready(k // 2)
                        last = product(pu[s][:, m, :], s, 2 * k + m, hi[:, k, :], lo[:, k, :], k == 0, k == NT - 1)
                last.then_inc(unit_done[s], 1)

            def sums(bank, src, wait, each=None):
                for t in range(NT):
                    if t % 2 == 0:
                        wait(t // 2)
                    last = MM(bank, ones[:, :], src[:, t, :], start=(t == 0), stop=(t == NT - 1))
                    if each is not None and t < len(each):
                        last.then_inc(each[t], 1)
                last.then_inc(stat_done, 1)

            pe.wait_ge(setup, 2)
            sums(po[:, 0, :], sq, lambda p: pe.wait_ge(sq_ready, p + 1), unit_done)
            pe.wait_ge(c_in, 16)
            swap, ident = const[:, C_SWAP:C_SWAP + P], const[:, C_ID:C_ID + P]

            with pe.Fori(0, DEPTH) as l:
                def standard(u, hi, lo, ready=None):
                    if u >= RING:
                        pe.wait_ge(*result_read(l, u - RING))
                    unit(u % RING, uses(l, u), hi, lo, ready)

                def parts_ready(high, high_before, low, low_before):
                    def ready(p):
                        pe.wait_ge(high, high_before + p + 1)
                        pe.wait_ge(low, low_before + p + 1)
                    return ready

                def swap_halves(n, src, tiles):
                    if n:
                        pe.wait_ge(rope_ab, l * 10 + 2 * n)
                    MM(pt[:, 0:tiles, :], swap, src, start=True, stop=True).then_inc(rot_done, 1)

                def scores(n):
                    c, g = n % N_CHUNKS, n // N_CHUNKS
                    keys = slice(max(c - 1, 0) * CHUNK, (c + 1) * CHUNK)
                    pe.wait_ge(rope_done, l * 10 + (6 if g == 0 else 10))
                    if n >= 2:
                        pe.wait_ge(exp_done, l * GROUPS + n - 1)
                    bank = ps[n % 2][:, :, :].rearrange("p a (b t) -> p (a b) t", t=P)
                    for j in range(GROUP_PAIRS):
                        last = MM(bank[:, j, 0:keys.stop - keys.start], qr[:, GROUP_PAIRS * g + j, c, :, :],
                                  kr[:, g, keys], start=True, stop=True)
                    last.then_inc(s_done, 1)

                def transpose_probs(n):
                    pe.wait_ge(p_ready, l * GROUPS + n + 1)
                    pe.wait_ge(rope_ab, l * 10 + 10)
                    if n:
                        pe.wait_ge(pt_ready, l * GROUPS + n)
                    bank = pt[:, :, :].rearrange("p a (b t) -> p (a b) t", t=P)
                    for j in range(GROUP_PAIRS):
                        last = nc.tensor.transpose(bank[:, j, :], probs[n % 2][:, j, :], ident)
                    last.then_inc(tr_done, 1)

                def values(n):
                    c, g = n % N_CHUNKS, n // N_CHUNKS
                    pe.wait_ge(v_ready, l * 2 + 2)
                    pe.wait_ge(pt_ready, l * GROUPS + n + 1)
                    if n:
                        pe.wait_ge(ol_ready, l * GROUPS + n)
                    MM(po[0:HEAD_DIM, :, :], vwin[:, c, HEAD_DIM * g:HEAD_DIM * g + HEAD_DIM], probsT[n % 2][:, :, :],
                       start=True, stop=True).then_inc(pv_done, 1)

                h_ready = parts_ready(hh_ready, l * 12, hl_ready, l * 12)
                for i in range(NT):
                    standard(U_GLU + i, hh, hl, h_ready if i == 0 else None)
                standard(U_KV, hh, hl)
                standard(U_Q, hh, hl)
                pe.wait_ge(kv_raw, l + 1)
                swap_halves(0, kvraw[:, 0:1, :], 1)
                windows = po[:, :, :].rearrange("p a (b t) -> p (a b) t", t=P)
                for c in range(1, N_CHUNKS):
                    nc.tensor.transpose(windows[:, c, :], kvraw[:, 1, CHUNK * (c - 1):CHUNK * (c + 1)], ident)
                nc.tensor.transpose(windows[0:CHUNK, 0, :], kvraw[:, 1, 0:CHUNK], ident).then_inc(vt_done, 1)
                for i in range(4):
                    if i < 3:
                        standard(U_Q + 1 + i, hh, hl)
                    else:
                        scores(0)
                        standard(U_GATE, hh, hl)
                    pe.wait_ge(q_raw, l * 4 + i + 1)
                    swap_halves(1 + i, qraw[i % 2], 2)
                for i in range(GROUPS):
                    if i:
                        standard(U_GATE + i, hh, hl)
                    if i + 1 < GROUPS:
                        scores(i + 1)
                    transpose_probs(i)
                    if i:
                        values(i - 1)
                values(GROUPS - 1)

                def o_ready(p):
                    pe.wait_ge(oh_ready, l * 2 * GROUPS + 2 * GROUPS)
                    pe.wait_ge(ol_ready, l * GROUPS + GROUPS)

                for i in range(2):
                    standard(U_AO + i, oh, ol, o_ready if i == 0 else None)
                sums(pt[:, 0, :], cv, lambda p: pe.wait_ge(conv_step, (l + 1) * 2 * CONV_STEPS) if p == 0 else None)
                standard(U_AO + 2, oh, ol)
                sums(ps[0][:, 0, :], sq, lambda p: pe.wait_ge(sq_ready, l * 12 + 4 + p + 1))
                standard(U_AO + 3, oh, ol)
                u_parts = parts_ready(uh_ready, l * 4, ul_ready, l * 4)
                for i in range(4):
                    standard(U_CO + i, uh, ul, u_parts if i == 0 else None)
                merged = parts_ready(hh_ready, l * 12 + 4, hl_ready, l * 12 + 4)
                for i in range(4):
                    standard(U_OUT + i, hh, hl, merged if i == 0 else None)
                sums(po[:, 0, :], sq, lambda p: pe.wait_ge(sq_ready, l * 12 + 8 + p + 1))
                h2_ready = parts_ready(hh_ready, l * 12 + 8, hl_ready, l * 12 + 8)
                standard(U_FFN, hh, hl, h2_ready)
                pe.wait_ge(down_zero, l + 1)
                standard(U_FFN + 1, hh, hl)

                def down_unit(s, k, parity):
                    for ab in range(2):
                        pe.wait_ge(fh_ready, k + ab + 1)
                        pe.wait_ge(fl_ready, k + ab + 1)
                        tile = 2 * parity + ab
                        for m in range(NT):
                            last = product(down[m // 2][:, m % 2, :], s, NT * ab + m, fh[:, tile, :], fl[:, tile, :], False, True, True)
                    last.then_inc(unit_done[s], 1)

                def ffn_step(j, parity):
                    k = j * 2 + l * FT
                    n = l * USES + j
                    pe.wait_ge(f_tap, 4 * k - 4)
                    unit(2, n + 10, hh, hl)
                    pe.wait_ge(f_tap, 4 * k)
                    unit(0, n + 11, hh, hl)
                    pe.wait_ge(hi_ready[1], n + 12)
                    pe.wait_ge(lo_ready[1], n + 12)
                    down_unit(1, k - 2, 1 - parity)

                with pe.Fori(0, FFN_STEPS // 2) as r:
                    ffn_step(r * 2 + 1, 1)
                    ffn_step(r * 2 + 2, 0)
                pe.wait_ge(hi_ready[2], (l + 1) * USES)
                pe.wait_ge(lo_ready[2], (l + 1) * USES)
                down_unit(2, l * FT + FT - 2, 0)
                sums(po[:, 0, :], sq, lambda p: pe.wait_ge(sq_ready, l * 12 + 12 + p + 1))


def kernel(**inputs):
    import numpy as np
    import concourse.bacc as bacc
    from concourse.bass_utils import run_bass_kernel_spmd

    a = {n: np.ascontiguousarray(v) for n, v in inputs.items()}

    def columns(v):
        v = v.reshape(v.shape[:-1] + (v.shape[-1] // P, P))
        return np.moveaxis(v, -1, 0)

    layers = []
    units = np.empty((DEPTH * UNITS, P, UNIT), np.float32)
    for l in range(DEPTH):
        p = np.empty((P, NPAR), np.float32)
        for at, name in ((PA_G, "attn_norm_g"), (PA_CB, "conv_dw_b"), (PA_LG, "conv_ln_g"), (PA_LB, "conv_ln_b"), (PA_FG, "ffn_norm_g")):
            p[:, at:at + NT] = columns(a[name][l])
        p[:, PA_CW:PA_SINK] = columns(a["conv_dw_w"][l]).transpose(0, 2, 1).reshape(P, -1)
        p[:, PA_SINK:PA_FW] = np.repeat(a["attn_sinks"][l].reshape(N_PAIRS, 2).T, HEAD_DIM, axis=0)
        taps = columns(np.concatenate([a["ffn_dw_w"][l], a["ffn_dw_b"][l][None]]))
        p[:, PA_FW:] = taps.transpose(0, 2, 1).reshape(P, -1)
        layers.append(p)

        w_in = a["w_in"][l].reshape(NT, P, -1, P)
        kv, q, glu, gates = 8, 0, 10, 26
        order = [(w_in, glu + i, glu + NT + i) for i in range(NT)] + [(w_in, kv, kv + 1)]
        order += [(w_in, q + 2 * i, q + 2 * i + 1) for i in range(4)]
        order += [(w_in, gates + i, gates + NT + i) for i in range(NT)]
        for name in ("w_attn_o", "w_conv_o", "w_out"):
            w = a[name][l].reshape(NT, P, -1, P)
            order += [(w, 2 * i, 2 * i + 1) for i in range(4)]
        up = a["w_ffn_up"][l].reshape(NT, P, -1, P)
        ups = [(up, i, FT + i) for i in range(FT)]
        down = a["w_ffn_down"][l].reshape(FFN_STEPS, 2, P, D_MODEL)
        order += ups[0:2]
        for j in range(1, FFN_STEPS):
            order += [ups[2 * j], ups[2 * j + 1], down[j - 1]]
        order += [down[FFN_STEPS - 1]]
        for n, item in enumerate(order):
            if isinstance(item, tuple):
                w, c0, c1 = item
                block = w[:, :, [c0, c1], :].transpose(1, 0, 2, 3)
            else:
                block = item.transpose(1, 0, 2)
            units[l * UNITS + n] = block.reshape(P, UNIT)

    const = np.zeros((P, NCONST), np.float32)
    d = np.arange(P)
    const[:, C_FREQ] = THETA ** (-(d % 32) / 32.0)
    const[d ^ 32, C_SWAP + d] = np.where(d % 64 < 32, -1.0, 1.0)
    const[d, C_ID + d] = 1.0
    const[:, C_EPS], const[:, C_HALFPI] = EPS, np.pi / 2

    arrays = {
        "x_t": np.ascontiguousarray(columns(a["x"][0]).transpose(0, 2, 1)),
        "positions": a["positions"].reshape(1, SEQ) if a["positions"].dtype == np.int32 else a["positions"],
        "const": const,
        "params": np.ascontiguousarray(np.concatenate(layers, axis=1)),
        "final_g": np.ascontiguousarray(columns(a["final_norm_g"])),
        "weights": units,
    }
    nc = bacc.Bacc("TRN2", target_bir_lowering=False, num_devices=1)
    args = [nc.dram_tensor("in_" + n, v.shape, mybir.dt.from_np(v.dtype), kind="ExternalInput").ap() for n, v in arrays.items()]
    out = nc.dram_tensor("out_y", (P, NT, SEQ), mybir.dt.float32, kind="ExternalOutput").ap()
    hybrid_encoder(nc, *args, out)
    r = run_bass_kernel_spmd(nc, [{"in_" + n: v for n, v in arrays.items()}], core_ids=[0])
    y = r.results[0]["out_y"]
    return np.ascontiguousarray(y.transpose(2, 1, 0)).reshape(1, SEQ, D_MODEL)
```

```python
import concourse.bass as bass
from concourse import mybir
from contextlib import ExitStack

DEPTH, D_MODEL, SEQ = 2, 1024, 256
CHUNK, HEAD_DIM, N_HEADS, N_KV = 64, 64, 16, 2
CONV_WIDTH, D_FF = 31, 2816
THETA, EPS = 10000.0, 1e-5
P = 128
NT = D_MODEL // P
T = SEQ
FT = D_FF // P
N_CHUNKS = SEQ // CHUNK
N_PAIRS = N_HEADS // 2
GROUPS = N_CHUNKS * N_KV
GROUP_PAIRS = N_PAIRS // N_KV

BLOCKS = 16
UNIT = BLOCKS * P
RING = 3
U_GLU, U_KV, U_Q, U_GATE = 0, 8, 9, 13
U_AO, U_CO, U_OUT, U_FFN = 21, 25, 29, 33
FFN_STEPS = FT // 2
UNITS = U_FFN + 3 * FFN_STEPS
AHEAD = 2
USES = UNITS // RING

PA_G, PA_CB, PA_LG, PA_LB, PA_FG = 0, 8, 16, 24, 32
PA_CW = 40
PA_SINK = PA_CW + NT * CONV_WIDTH
PA_FW = PA_SINK + N_PAIRS
NPAR = PA_FW + 2 * FT * 4
C_FREQ, C_EPS, C_HALFPI, C_SWAP, C_ID = 0, 1, 2, 4, 132
NCONST = 260

TAPS = CONV_WIDTH - 1
CONV_STEPS = TAPS * NT // 2
ROUNDING = 1.5 * 2.0 ** 23
PI_BELOW = 3.1415925
ANGLE_SCALES = (2 ** 20, 2 ** 10, 1)
TABLE_STEPS = 4 + 5 * len(ANGLE_SCALES)


def pi_parts(scale):
    import numpy as np
    rest, parts = np.float64(2 * np.pi * scale), []
    for _ in range(2):
        unit = 2.0 ** (np.floor(np.log2(rest)) - 11)
        parts.append(float(np.floor(rest / unit) * unit))
        rest = rest - parts[-1]
    return parts + [float(np.float32(rest))]


def hybrid_encoder(nc, x_in, pos_in, const_in, par_in, gf_in, w_in, y_out):
    f32, f32r, i32 = mybir.dt.float32, mybir.dt.float32r, mybir.dt.int32
    ALU, ACT, AX = mybir.AluOpType, mybir.ActivationFunctionType, mybir.AxisListType
    ctx = ExitStack()
    with ctx:
        def sb(name, shape, dt=f32):
            return ctx.enter_context(nc.sbuf_tensor(name, shape, dt))

        def pb(name):
            return ctx.enter_context(nc.psum_tensor(name, [P, 2, T], f32))

        def sem(name):
            return ctx.enter_context(nc.semaphore(name))

        raw = [sb(f"raw{s}", [P, UNIT]) for s in range(RING)]
        whi = [sb(f"whi{s}", [P, UNIT], f32r) for s in range(RING)]
        wlo = [sb(f"wlo{s}", [P, UNIT], f32r) for s in range(RING)]
        x = sb("x", [P, NT, T])
        hh, hl = sb("hh", [P, NT, T], f32r), sb("hl", [P, NT, T], f32r)
        oh, ol = sb("oh", [P, NT, T], f32r), sb("ol", [P, NT, T], f32r)
        uh, ul = sb("uh", [P, NT, T], f32r), sb("ul", [P, NT, T], f32r)
        fh, fl = oh[:, 0:4, :], ol[:, 0:4, :]
        const = sb("const", [P, NCONST])
        ones = sb("ones", [P, P])
        par_all = sb("par_all", [P, DEPTH * NPAR])
        par = sb("par", [P, NPAR])
        gf = sb("gf", [P, NT])
        cos, sin = sb("cos", [P, T]), sb("sin", [P, T])
        upad = sb("upad", [P, NT, CONV_WIDTH - 1 + T])
        cv = sb("cv", [P, NT, T])
        gate = sb("gate", [P, 2, NT, T])
        qk = sb("qk", [P, 4096])
        qr = qk[0:HEAD_DIM, :].rearrange("p (i c o t) -> p i c o t", i=N_PAIRS, c=N_CHUNKS, o=2)
        sq = qk[:, 0:2048].rearrange("p (n t) -> p n t", n=NT)
        h32 = qk[:, 2048:4096].rearrange("p (n t) -> p n t", n=NT)
        fbuf = qk[:, 2048:4096].rearrange("p (a n t) -> p a n t", a=2, n=4)
        kvraw = sb("kvraw", [P, 2, T])
        kr = sb("kr", [HEAD_DIM, N_KV, T])
        vwin = sb("vwin", [P, N_CHUNKS, P])
        probs = [sb(f"probs{i}", [P, GROUP_PAIRS, P]) for i in range(2)]
        probsT = [sb(f"probsT{i}", [P, GROUP_PAIRS, P]) for i in range(2)]
        small = sb("small", [P, 2, 8, GROUP_PAIRS])
        less_sink = sb("less_sink", [P, N_PAIRS])
        lnv, rstd, warm = sb("lnv", [P, T]), sb("rstd", [P, T]), sb("warm", [P, 1])
        qraw = [gate[:, 0, 4 + 2 * i:6 + 2 * i, :] for i in range(2)]
        rope_a, rope_b = gate[:, 1, 4:6, :], gate[:, 1, 6:8, :]
        up = gate[:, 0, 0:4, :].rearrange("p (a n) t -> p a n t", a=2)

        pos_i, turns = probs[0][:, 0:2, :].bitcast(i32), probsT[0][:, 2:4, :]
        ang, aabs = sb("ang", [P, 2, P])[:, :, :], sb("aabs", [P, 2, P])[:, :, :]

        pu = [pb(f"pu{s}") for s in range(RING)]
        ps = [pb(f"ps{i}") for i in range(2)]
        pt, po, pc = pb("pt"), pb("po"), pb("pc")
        down = [ps[0], ps[1], pt, pc]

        raw_in = [sem(f"raw_in{s}") for s in range(RING)]
        hi_ready = [sem(f"hi_ready{s}") for s in range(RING)]
        lo_ready = [sem(f"lo_ready{s}") for s in range(RING)]
        unit_done = [sem(f"unit_done{s}") for s in range(RING)]
        x_in_s = [sem(f"x_in{half}") for half in range(2)]
        c_in, pos_s, par_in_s = sem("const_in"), sem("pos_in"), sem("par_in")
        setup, table, act_table = sem("setup"), sem("table"), sem("act_table")
        par_ready, pad_zero = sem("par_ready"), sem("pad_zero")
        sq_ready, stat_done, ln_done, rstd_ready = sem("sq_ready"), sem("stat_done"), sem("ln_done"), sem("rstd_ready")
        h32_ready, hh_ready, hl_ready, x_ready = sem("h32_ready"), sem("hh_ready"), sem("hl_ready"), sem("x_ready")
        glu_tanh, u_ready, conv_first, conv_step = sem("glu_tanh"), sem("u_ready"), sem("conv_first"), sem("conv_step")
        kv_raw, q_raw, rot_done, rope_ab, rope_done = sem("kv_raw"), sem("q_raw"), sem("rot_done"), sem("rope_ab"), sem("rope_done")
        vt_done, v_ready = sem("vt_done"), sem("v_ready")
        s_done, mx_step, exp_done, den_step, p_ready = sem("s_done"), sem("mx_step"), sem("exp_done"), sem("den_step"), sem("p_ready")
        tr_done, pt_ready, pv_done, oh_ready, ol_ready = sem("tr_done"), sem("pt_ready"), sem("pv_done"), sem("oh_ready"), sem("ol_ready")
        xc_ready, t_ready, silu_ready, uh_ready, ul_ready = sem("xc_ready"), sem("t_ready"), sem("silu_ready"), sem("uh_ready"), sem("ul_ready")
        gate_ready, m_step = sem("gate_ready"), sem("m_step")
        down_zero, down_done, up_ready, f_conv0, f_tap, f_silu, f_ready, fh_ready, fl_ready = [
            sem(n) for n in ("down_zero", "down_done", "up_ready", "f_conv0", "f_tap", "f_silu", "f_ready", "fh_ready", "fl_ready")]
        y_ready, y_out_s = sem("y_ready"), sem("y_out")

        def uses(l, u):
            return l * USES + u // RING

        def result_read(l, u):
            if u < U_KV:
                return u_ready, l * NT + u + 1
            if u < U_Q:
                return kv_raw, l + 1
            if u < U_GATE:
                return q_raw, l * 4 + u - U_Q + 1
            if u < U_AO:
                return gate_ready, l * NT + u - U_GATE + 1
            if u < U_CO:
                return m_step, l * 12 + u - U_AO + 1
            if u < U_OUT:
                return m_step, l * 12 + 4 + 2 * (u - U_CO) + 1
            return x_ready, l * 8 + u - U_OUT + 1

        block = ctx.enter_context(nc.Block())

        @block.sync
        def _(sp):
            for half in range(2):
                tiles = slice(NT // 2 * half, NT // 2 * half + NT // 2)
                sp.dma_start(x[:, tiles, :], x_in[:, tiles, :]).then_inc(x_in_s[half], 16)
            def load_unit(s, at):
                sp.dma_start(raw[s][:, :], w_in[at, :, :].rearrange("a p n -> p (a n)")).then_inc(raw_in[s], 16)

            for s in range(RING):
                load_unit(s, slice(s, s + 1))
            with sp.Fori(1, DEPTH * USES) as r:
                for s in range(RING):
                    sp.wait_ge(lo_ready[s], r)
                    load_unit(s, bass.ds(r * RING + s, 1))
            for s in range(AHEAD):
                sp.wait_ge(lo_ready[s], DEPTH * USES)
                load_unit(s, slice(DEPTH * UNITS + s, DEPTH * UNITS + s + 1))
            for half in range(2):
                sp.wait_ge(y_ready, NT // 2 * (half + 1))
                sp.dma_start(y_out[:, 4 * half:4 * half + 4, :], h32[:, 4 * half:4 * half + 4, :]).then_inc(y_out_s, 16)
            sp.wait_ge(y_out_s, 32)

        @block.gpsimd
        def _(pool):
            nc.gpsimd.memset(ones[:, :], 1.0 / D_MODEL).then_inc(setup, 1)
            nc.gpsimd.memset(upad[:, :, 0:CONV_WIDTH - 1], 0.0).then_inc(pad_zero, 1)
            def split_low(s, n):
                pool.wait_ge(hi_ready[s], n + 1)
                nc.gpsimd.tensor_tensor(wlo[s][:, :], raw[s][:, :], whi[s][:, :].bitcast(f32), ALU.subtract).then_inc(lo_ready[s], 1)

            for s in range(AHEAD):
                split_low(s, 0)
            with pool.Fori(0, DEPTH) as l:
                split_low(2, l * USES)
                with pool.Fori(1, U_FFN // RING) as r:
                    for s in range(RING):
                        split_low(s, l * USES + r)
                with pool.Fori(12, USES) as n:
                    split_low(1, l * USES + n)
                for s in range(AHEAD):
                    split_low(s, l * USES + USES)

        @block.scalar
        def _(act):
            A = nc.scalar.activation
            act.dma_start(pos_i, pos_in.partition_broadcast(P)).then_inc(pos_s, 16)
            act.dma_start(const[:, :], const_in).then_inc(c_in, 16)
            act.dma_start(par_all[:, :], par_in).then_inc(par_in_s, 16)
            act.dma_start(gf[:, :], gf_in).then_inc(par_in_s, 16)

            def split_high(l, s, n):
                act.wait_ge(raw_in[s], (l * USES + n + 1) * 16)
                act.wait_ge(unit_done[s], l * USES + n + 1)
                A(whi[s][:, :], raw[s][:, :], ACT.Copy).then_inc(hi_ready[s], 1)

            def next_high(l, u):
                if u + RING < UNITS:
                    split_high(l, (u + RING) % RING, (u + RING) // RING)

            def inverse_root(bank, stats, roots):
                A(warm[:, :], const[:, C_EPS:C_EPS + 1], ACT.Ln)
                act.wait_ge(stat_done, stats)
                A(lnv[:, :], bank, ACT.Ln, bias=const[:, C_EPS:C_EPS + 1]).then_inc(ln_done, 1)
                act.wait_ge(ln_done, roots)
                A(rstd[:, :], lnv[:, :], ACT.Exp, scale=-0.5).then_inc(rstd_ready, 1)

            def high_pair(high, ready, before, p):
                act.wait_ge(h32_ready, before + 2 * p + 2)
                A(high[:, 2 * p:2 * p + 2, :], h32[:, 2 * p:2 * p + 2, :], ACT.Copy).then_inc(ready, 1)

            for p in range(NT // 2):
                act.wait_ge(x_in_s[p // 2], 16)
                A(sq[:, 2 * p:2 * p + 2, :], x[:, 2 * p:2 * p + 2, :], ACT.Square).then_inc(sq_ready, 1)
            act.wait_ge(c_in, 16)
            split_high(0, 0, 0)
            inverse_root(po[:, 0, :], 1, 1)
            split_high(0, 1, 0)

            with act.Fori(0, DEPTH) as l:
                for p in range(NT // 2):
                    high_pair(hh, hh_ready, l * 2 * NT, p)
                split_high(l, 2, 0)
                def first_tap(t):
                    act.wait_ge(u_ready, l * NT + t + 1)
                    w = PA_CW + t * CONV_WIDTH
                    A(cv[:, t, :], upad[:, t, 0:T], ACT.Identity, scale=par[:, w:w + 1],
                      bias=par[:, PA_CB + t:PA_CB + t + 1]).then_inc(conv_first, 1)

                for i in range(NT):
                    u = U_GLU + i
                    act.wait_ge(unit_done[u % RING], uses(l, u) + 2)
                    if i >= 2:
                        act.wait_ge(u_ready, l * NT + i - 1)
                    A(kvraw[:, i % 2, :], pu[u % RING][:, 1, :], ACT.Tanh, scale=0.5).then_inc(glu_tanh, 1)
                    if i >= 1:
                        first_tap(i - 1)
                    if i == 2:
                        act.wait_ge(table, TABLE_STEPS)
                        A(sin[:, :], ang, ACT.Sin).then_inc(act_table, 1)
                        A(cos[:, :], aabs, ACT.Sin, scale=-1.0, bias=const[:, C_HALFPI:C_HALFPI + 1]).then_inc(act_table, 1)
                    next_high(l, u)
                first_tap(NT - 1)
                u = U_KV
                act.wait_ge(unit_done[u % RING], uses(l, u) + 2)
                act.wait_ge(u_ready, l * NT + NT)
                A(kvraw[:, :, :], pu[u % RING][:, :, :], ACT.Copy).then_inc(kv_raw, 1)
                next_high(l, u)
                for i in range(4):
                    u = U_Q + i
                    act.wait_ge(unit_done[u % RING], uses(l, u) + 2)
                    if i >= 2:
                        act.wait_ge(rope_done, l * 10 + 2 * i)
                    A(qraw[i % 2], pu[u % RING][:, :, :], ACT.Copy).then_inc(q_raw, 1)
                    if i == 1:
                        act.wait_ge(vt_done, l + 1)
                        A(vwin[0:CHUNK, 0, :], po[0:CHUNK, 0, 0:P], ACT.Copy).then_inc(v_ready, 1)
                        A(vwin[:, 1:N_CHUNKS, :], po[:, :, :].rearrange("p a (b t) -> p (a b) t", t=P)[:, 1:N_CHUNKS, :], ACT.Copy).then_inc(v_ready, 1)
                    next_high(l, u)

                def evict_transposed(n):
                    act.wait_ge(tr_done, l * GROUPS + n + 1)
                    A(probsT[n % 2][:, :, :], pt[:, :, :].rearrange("p a (b t) -> p (a b) t", t=P), ACT.Copy).then_inc(pt_ready, 1)

                def high_of_o(n):
                    c, g = n % N_CHUNKS, n // N_CHUNKS
                    act.wait_ge(pv_done, l * GROUPS + n + 1)
                    src = po[0:HEAD_DIM, :, :].rearrange("p a (b h t) -> p (a b) h t", b=2, h=2)
                    for odd in range(2):
                        A(oh[64 * odd:64 * odd + 64, 4 * g:4 * g + 4, CHUNK * c:CHUNK * c + CHUNK], src[:, :, odd, :], ACT.Copy).then_inc(oh_ready, 1)

                def exps(n):
                    keys = CHUNK if n % N_CHUNKS == 0 else P
                    g = n // N_CHUNKS
                    act.wait_ge(mx_step, (l * GROUPS + n) * 3 + 3)
                    scores = ps[n % 2][:, :, :].rearrange("p a (b t) -> p (a b) t", t=P)
                    sm = small[:, n % 2, :, :]
                    A(sm[:, 4, :], sm[:, 3, :], ACT.Exp)
                    for j in range(GROUP_PAIRS):
                        last = A(probs[n % 2][:, j, 0:keys], scores[:, j, 0:keys], ACT.Exp, scale=HEAD_DIM ** -0.5,
                                 bias=sm[:, 2, j:j + 1], accum_out=sm[:, 5, j:j + 1])
                    last.then_inc(exp_done, 1)

                def probabilities(n):
                    keys = CHUNK if n % N_CHUNKS == 0 else P
                    act.wait_ge(den_step, (l * GROUPS + n) * 2 + 2)
                    for j in range(GROUP_PAIRS):
                        pr = probs[n % 2][:, j, 0:keys]
                        last = A(pr, pr, ACT.Copy, scale=small[:, n % 2, 7, j:j + 1])
                    last.then_inc(p_ready, 1)

                for i in range(NT):
                    u = U_GATE + i
                    if i >= 1:
                        evict_transposed(i - 1)
                    exps(i)
                    if i >= 2:
                        high_of_o(i - 2)
                    probabilities(i)
                    if i == 4:
                        act.wait_ge(rope_done, l * 10 + 10)
                    act.wait_ge(unit_done[u % RING], uses(l, u) + 2)
                    A(gate[:, :, i, :], pu[u % RING][:, :, :], ACT.Tanh, scale=0.5).then_inc(gate_ready, 1)
                    if i < NT - 1:
                        next_high(l, u)
                evict_transposed(GROUPS - 1)
                high_of_o(GROUPS - 2)
                high_of_o(GROUPS - 1)
                next_high(l, U_AO - 1)
                next_high(l, U_AO)
                next_high(l, U_AO + 1)
                for p in range(NT // 2):
                    act.wait_ge(xc_ready, l * 4 + p + 1)
                    A(sq[:, 2 * p:2 * p + 2, :], cv[:, 2 * p:2 * p + 2, :], ACT.Square).then_inc(sq_ready, 1)
                next_high(l, U_AO + 2)
                inverse_root(ps[1][:, 0, :], l * 4 + 3, l * 3 + 2)
                for p in range(NT // 2):
                    act.wait_ge(t_ready, l * 4 + p + 1)
                    for t in (2 * p, 2 * p + 1):
                        last = A(cv[:, t, :], cv[:, t, :], ACT.Silu, scale=par[:, PA_LG + t:PA_LG + t + 1],
                                 bias=par[:, PA_LB + t:PA_LB + t + 1])
                    last.then_inc(silu_ready, 1)
                next_high(l, U_AO + 3)
                for i in range(4):
                    act.wait_ge(m_step, l * 12 + 4 + 2 * i + 2)
                    A(hh[:, 2 * i:2 * i + 2, :], gate[:, 1, 2 * i:2 * i + 2, :], ACT.Copy, scale=0.5).then_inc(hh_ready, 1)
                    next_high(l, U_CO + i)
                for i in range(4):
                    act.wait_ge(x_ready, l * 8 + i + 1)
                    A(sq[:, 2 * i:2 * i + 2, :], x[:, 2 * i:2 * i + 2, :], ACT.Square).then_inc(sq_ready, 1)
                    high_pair(uh, uh_ready, l * 2 * NT + NT, i)
                    next_high(l, U_OUT + i)
                inverse_root(po[:, 0, :], l * 4 + 4, l * 3 + 3)

                def hidden_tile(k, ab, gcol, vcol, before=None, split=None):
                    act.wait_ge(up_ready, k + 1)
                    if before is not None:
                        act.wait_ge(f_ready, before)
                    for half, col in ((0, gcol), (1, vcol)):
                        A(fbuf[:, ab, half, :], up[:, ab, half, :], ACT.Identity, scale=par[:, bass.ds(col + 2, 1)],
                          bias=par[:, bass.ds(col + 3, 1)]).then_inc(f_conv0, 1)
                    if split is not None:
                        split()
                    act.wait_ge(f_tap, k * 4 + 3)
                    A(fbuf[:, ab, 2, :], fbuf[:, ab, 0, :], ACT.Silu).then_inc(f_silu, 1)

                def hidden_high(k, ab, parity):
                    act.wait_ge(f_ready, k + 1)
                    A(fh[:, 2 * parity + ab, :], fbuf[:, ab, 3, :], ACT.Copy).then_inc(fh_ready, 1)

                base = l * FT
                hidden_tile(base, 0, PA_FW, PA_FW + FT * 4, None, lambda: next_high(l, U_FFN))
                hidden_high(base, 0, 0)
                hidden_tile(base + 1, 1, PA_FW + 4, PA_FW + FT * 4 + 4, None, lambda: next_high(l, U_FFN + 1))
                hidden_high(base + 1, 1, 0)

                def ffn_step(j, parity, last):
                    k = j * 2 + l * FT
                    col = j * 8 + PA_FW
                    hidden_tile(k, 0, col, col + FT * 4, k - 1, lambda: split_high(l, 2, j + 11))
                    act.wait_ge(unit_done[1], l * USES + j + 12)
                    hidden_high(k, 0, parity)
                    hidden_tile(k + 1, 1, col + 4, col + FT * 4 + 4, k, None if last else lambda: split_high(l, 0, j + 12))
                    hidden_high(k + 1, 1, parity)
                    if not last:
                        split_high(l, 1, j + 12)

                with act.Fori(0, FFN_STEPS // 2 - 1) as r:
                    ffn_step(r * 2 + 1, 1, False)
                    ffn_step(r * 2 + 2, 0, False)
                ffn_step(FFN_STEPS - 2, 1, False)
                ffn_step(FFN_STEPS - 1, 0, True)
                for s in range(AHEAD):
                    split_high(l, s, USES)
                for i in range(4):
                    act.wait_ge(x_ready, l * 8 + 4 + i + 1)
                    A(sq[:, 2 * i:2 * i + 2, :], x[:, 2 * i:2 * i + 2, :], ACT.Square).then_inc(sq_ready, 1)
                inverse_root(po[:, 0, :], l * 4 + 5, l * 3 + 4)

        @block.vector
        def _(dve):
            V = nc.vector
            V.memset(vwin[CHUNK:P, 0, :], 0.0).then_inc(setup, 1)
            done = [0]

            def step(instruction):
                done[0] += 1
                instruction.then_inc(table, 1)
                dve.wait_ge(table, done[0])

            dve.wait_ge(pos_s, 16)
            dve.wait_ge(c_in, 16)
            step(V.tensor_copy(ang, pos_i))
            step(V.tensor_scalar(ang, ang, const[:, C_FREQ:C_FREQ + 1], None, ALU.mult))
            for scale in ANGLE_SCALES:
                parts = pi_parts(scale)
                step(V.tensor_scalar(turns, ang, 1.0 / sum(parts), ROUNDING, ALU.mult, ALU.add))
                step(V.tensor_scalar(turns, turns, -ROUNDING, None, ALU.add))
                for part in parts:
                    step(V.scalar_tensor_tensor(ang, turns, -part, ang, ALU.mult, ALU.add))
            step(V.tensor_scalar(ang, ang, PI_BELOW, -PI_BELOW, ALU.min, ALU.max))
            step(V.scalar_tensor_tensor(aabs, ang, -1.0, ang, ALU.mult, ALU.max))
            assert done[0] == TABLE_STEPS
            dve.wait_ge(par_in_s, 32)

            def normalise(l, gain, before, roots, hh_before):
                dve.wait_ge(rstd_ready, roots)

                def low(p):
                    dve.wait_ge(hh_ready, hh_before + p + 1)
                    V.tensor_tensor(hl[:, 2 * p:2 * p + 2, :], h32[:, 2 * p:2 * p + 2, :],
                                    hh[:, 2 * p:2 * p + 2, :].bitcast(f32), ALU.subtract).then_inc(hl_ready, 1)

                for p in range(NT // 2):
                    for t in (2 * p, 2 * p + 1):
                        V.scalar_tensor_tensor(h32[:, t, :], x[:, t, :], gain[:, t:t + 1], rstd[:, :],
                                               ALU.mult, ALU.mult).then_inc(h32_ready, 1)
                    if p:
                        low(p - 1)
                low(NT // 2 - 1)

            with dve.Fori(0, DEPTH) as l:
                V.tensor_copy(par[:, :], par_all[:, bass.ds(l * NPAR, NPAR)]).then_inc(par_ready, 1)
                dve.wait_ge(par_ready, l * 3 + 1)
                V.tensor_scalar(par[:, PA_CW:PA_CW + NT * CONV_WIDTH], par[:, PA_CW:PA_CW + NT * CONV_WIDTH], 0.5, None, ALU.mult).then_inc(par_ready, 1)
                V.tensor_scalar(less_sink[:, :], par[:, PA_SINK:PA_SINK + N_PAIRS], -1.0, None, ALU.mult).then_inc(par_ready, 1)
                normalise(l, par[:, PA_G:PA_G + NT], l * 2 * NT, l * 3 + 1, l * 8)
                dve.wait_ge(pad_zero, 1)
                dve.wait_ge(par_ready, l * 3 + 3)

                def glu(i):
                    u = U_GLU + i
                    dve.wait_ge(glu_tanh, l * NT + i + 1)
                    V.scalar_tensor_tensor(upad[:, i, CONV_WIDTH - 1:], kvraw[:, i % 2, :], 1.0, pu[u % RING][:, 0, :],
                                           ALU.add, ALU.mult).then_inc(u_ready, 1)

                def conv(first, last):
                    for n in range(first, last):
                        pair, k = n // TAPS, n % TAPS + 1
                        for j in range(2):
                            t = 2 * pair + j
                            w = par[:, PA_CW + t * CONV_WIDTH + k:PA_CW + t * CONV_WIDTH + k + 1]
                            if k == 1:
                                dve.wait_ge(conv_first, l * NT + t + 1)
                            if n:
                                dve.wait_ge(conv_step, l * 2 * CONV_STEPS + 2 * n + j - 1)
                            V.scalar_tensor_tensor(cv[:, t, :], upad[:, t, k:k + T], w, cv[:, t, :], ALU.mult, ALU.add).then_inc(conv_step, 1)

                glu(0)
                glu(1)
                for i in range(2, NT):
                    conv(6 * (i - 2), 6 * (i - 1))
                    glu(i)
                conv(36, 42)

                def rotate(n, src, tiles, outs):
                    a, b = rope_a[:, 0:tiles, :], rope_b[:, 0:tiles, :]
                    c = cos[:, :].unsqueeze(1).to_broadcast([P, tiles, T])
                    s = sin[:, :].unsqueeze(1).to_broadcast([P, tiles, T])
                    if n:
                        dve.wait_ge(rope_done, l * 10 + 2 * n)
                    V.tensor_tensor(a, src, c, ALU.mult).then_inc(rope_ab, 1)
                    dve.wait_ge(rot_done, l * 5 + n + 1)
                    V.tensor_tensor(b, pt[:, 0:tiles, :], s, ALU.mult).then_inc(rope_ab, 1)
                    dve.wait_ge(rope_ab, l * 10 + 2 * n + 2)
                    for odd in range(2):
                        rows = slice(64 * odd, 64 * odd + 64)
                        split = [v[rows].rearrange("p n (c t) -> p n c t", c=N_CHUNKS) for v in (a, b)]
                        V.tensor_tensor(outs[odd], split[0], split[1], ALU.add).then_inc(rope_done, 1)

                dve.wait_ge(act_table, l * 2 + 2)
                dve.wait_ge(kv_raw, l + 1)
                rotate(0, kvraw[:, 0:1, :], 1, [kr[:, g:g + 1, :].rearrange("p n (c t) -> p n c t", c=N_CHUNKS) for g in range(N_KV)])
                conv(42, 46)
                for i in range(4):
                    dve.wait_ge(q_raw, l * 4 + i + 1)
                    rotate(1 + i, qraw[i % 2], 2, [qr[:, 2 * i:2 * i + 2, :, odd, :] for odd in range(2)])
                    if i < 3:
                        conv(46 + 4 * i, 50 + 4 * i)

                def maxima(n):
                    g = n // N_CHUNKS
                    keys = CHUNK if n % N_CHUNKS == 0 else P
                    scores = ps[n % 2][:, :, :].rearrange("p a (b t) -> p (a b) t", t=P)[:, :, 0:keys]
                    sm = small[:, n % 2, :, :]
                    first = (l * GROUPS + n) * 3
                    dve.wait_ge(s_done, l * GROUPS + n + 1)
                    V.tensor_reduce(sm[:, 0, :], scores, AX.X, ALU.max).then_inc(mx_step, 1)
                    dve.wait_ge(mx_step, first + 1)
                    V.scalar_tensor_tensor(sm[:, 2, :], sm[:, 0, :], -(HEAD_DIM ** -0.5), less_sink[:, 4 * g:4 * g + 4],
                                           ALU.mult, ALU.min).then_inc(mx_step, 1)
                    dve.wait_ge(mx_step, first + 2)
                    V.tensor_tensor(sm[:, 3, :], sm[:, 2, :], par[:, PA_SINK + 4 * g:PA_SINK + 4 * g + 4], ALU.add).then_inc(mx_step, 1)

                def denominators(n):
                    keys = CHUNK if n % N_CHUNKS == 0 else P
                    sm = small[:, n % 2, :, :]
                    first = (l * GROUPS + n) * 2
                    dve.wait_ge(exp_done, l * GROUPS + n + 1)
                    V.tensor_tensor(sm[:, 6, :], sm[:, 5, :], sm[:, 4, :], ALU.add).then_inc(den_step, 1)
                    dve.wait_ge(den_step, first + 1)
                    if keys < P:
                        V.memset(probs[n % 2][:, :, keys:P], 0.0)
                    V.reciprocal(sm[:, 7, :], sm[:, 6, :]).then_inc(den_step, 1)

                def low_of_o(n):
                    c, g = n % N_CHUNKS, n // N_CHUNKS
                    src = po[0:HEAD_DIM, :, :].rearrange("p a (b h t) -> p (a b) h t", b=2, h=2)
                    dve.wait_ge(oh_ready, (l * GROUPS + n) * 2 + 2)
                    for odd in range(2):
                        at = (slice(64 * odd, 64 * odd + 64), slice(4 * g, 4 * g + 4), slice(CHUNK * c, CHUNK * c + CHUNK))
                        last = V.tensor_tensor(ol[at], src[:, :, odd, :], oh[at].bitcast(f32), ALU.subtract)
                    last.then_inc(ol_ready, 1)

                step_now = 58
                for i in range(GROUPS):
                    taps = (3, 4) if i < GROUPS - 2 else (2, 2)
                    maxima(i)
                    conv(step_now, step_now + taps[0])
                    denominators(i)
                    conv(step_now + taps[0], step_now + sum(taps))
                    step_now += sum(taps)
                    if i >= 2:
                        low_of_o(i - 2)
                low_of_o(GROUPS - 2)
                low_of_o(GROUPS - 1)

                def merge_attention(i):
                    u = U_AO + i
                    dve.wait_ge(gate_ready, l * NT + NT)
                    dve.wait_ge(unit_done[u % RING], uses(l, u) + 2)
                    g0 = gate[:, 0, 2 * i:2 * i + 2, :]
                    V.scalar_tensor_tensor(g0, g0, 1.0, pu[u % RING][:, :, :], ALU.add, ALU.mult).then_inc(m_step, 1)

                conv(step_now, CONV_STEPS)
                merge_attention(0)
                merge_attention(1)
                dve.wait_ge(stat_done, l * 4 + 2)
                for p in range(NT // 2):
                    c2 = cv[:, 2 * p:2 * p + 2, :]
                    V.tensor_tensor(c2, c2, ps[0][:, 0, :].unsqueeze(1).to_broadcast([P, 2, T]), ALU.subtract).then_inc(xc_ready, 1)
                merge_attention(2)
                dve.wait_ge(rstd_ready, l * 3 + 2)
                for p in range(NT // 2):
                    c2 = cv[:, 2 * p:2 * p + 2, :]
                    dve.wait_ge(xc_ready, l * 4 + p + 1)
                    V.tensor_tensor(c2, c2, rstd[:, :].unsqueeze(1).to_broadcast([P, 2, T]), ALU.mult).then_inc(t_ready, 1)
                for p in range(NT // 2):
                    dve.wait_ge(silu_ready, l * 4 + p + 1)
                    V.tensor_copy(uh[:, 2 * p:2 * p + 2, :], cv[:, 2 * p:2 * p + 2, :]).then_inc(uh_ready, 1)
                    dve.wait_ge(uh_ready, l * 8 + p + 1)
                    V.tensor_tensor(ul[:, 2 * p:2 * p + 2, :], cv[:, 2 * p:2 * p + 2, :], uh[:, 2 * p:2 * p + 2, :].bitcast(f32),
                                    ALU.subtract).then_inc(ul_ready, 1)
                merge_attention(3)
                for bank in down:
                    last = V.memset(bank[:, :, :], 0.0)
                last.then_inc(down_zero, 1)
                for i in range(4):
                    u = U_CO + i
                    dve.wait_ge(unit_done[u % RING], uses(l, u) + 2)
                    dve.wait_ge(m_step, l * 12 + 4 + 2 * i)
                    g1 = gate[:, 1, 2 * i:2 * i + 2, :]
                    V.scalar_tensor_tensor(g1, g1, 1.0, pu[u % RING][:, :, :], ALU.add, ALU.mult).then_inc(m_step, 1)
                    dve.wait_ge(m_step, l * 12 + 4 + 2 * i + 1)
                    V.tensor_tensor(g1, g1, gate[:, 0, 2 * i:2 * i + 2, :], ALU.add).then_inc(m_step, 1)
                    dve.wait_ge(hh_ready, l * 8 + 4 + i + 1)
                    V.scalar_tensor_tensor(hl[:, 2 * i:2 * i + 2, :], g1, 0.5, hh[:, 2 * i:2 * i + 2, :].bitcast(f32),
                                           ALU.mult, ALU.subtract).then_inc(hl_ready, 1)
                def split_low(s, n):
                    dve.wait_ge(hi_ready[s], l * USES + n + 1)
                    V.tensor_tensor(wlo[s][:, :], raw[s][:, :], whi[s][:, :].bitcast(f32), ALU.subtract).then_inc(lo_ready[s], 1)

                def input_low(p):
                    dve.wait_ge(uh_ready, l * 8 + 4 + p + 1)
                    V.tensor_tensor(ul[:, 2 * p:2 * p + 2, :], h32[:, 2 * p:2 * p + 2, :],
                                    uh[:, 2 * p:2 * p + 2, :].bitcast(f32), ALU.subtract).then_inc(ul_ready, 1)

                for i in range(4):
                    u = U_OUT + i
                    dve.wait_ge(unit_done[u % RING], uses(l, u) + 2)
                    x2 = x[:, 2 * i:2 * i + 2, :]
                    V.tensor_tensor(x2, pu[u % RING][:, :, :], x2, ALU.add).then_inc(x_ready, 1)
                    dve.wait_ge(x_ready, l * 8 + i + 1)
                    for t in (2 * i, 2 * i + 1):
                        V.tensor_scalar(h32[:, t, :], x[:, t, :], par[:, PA_FG + t:PA_FG + t + 1], None, ALU.mult).then_inc(h32_ready, 1)
                    input_low(i)
                    if i >= 2:
                        split_low(i - 2, 11)
                dve.wait_ge(rstd_ready, l * 3 + 3)

                def scale_up(s, ab, done_value):
                    dve.wait_ge(unit_done[s], done_value)
                    V.tensor_tensor(up[:, ab, :, :], pu[s][:, :, :], rstd[:, :].unsqueeze(1).to_broadcast([P, 2, T]),
                                    ALU.mult).then_inc(up_ready, 1)

                def hidden_tile(k, ab, gcol, vcol):
                    for m in range(4):
                        half, tap = m % 2, 1 - m // 2
                        shift = 2 - tap
                        if m < 2:
                            dve.wait_ge(f_conv0, k * 2 + 2)
                        else:
                            dve.wait_ge(f_tap, k * 4 + m - 1)
                        col = (gcol, vcol)[half] + tap
                        acc = fbuf[:, ab, half, shift:T]
                        last = V.scalar_tensor_tensor(acc, up[:, ab, half, 0:T - shift], par[:, bass.ds(col, 1)], acc,
                                                      ALU.mult, ALU.add).then_inc(f_tap, 1)
                    dve.wait_ge(f_tap, k * 4 + 4)
                    dve.wait_ge(f_silu, k + 1)
                    V.tensor_tensor(fbuf[:, ab, 3, :], fbuf[:, ab, 2, :], fbuf[:, ab, 1, :], ALU.mult).then_inc(f_ready, 1)

                def hidden_low(k, ab, parity):
                    dve.wait_ge(fh_ready, k + 1)
                    V.tensor_tensor(fl[:, 2 * parity + ab, :], fbuf[:, ab, 3, :], fh[:, 2 * parity + ab, :].bitcast(f32), ALU.subtract).then_inc(fl_ready, 1)

                k0 = l * FT
                scale_up(0, 0, uses(l, U_FFN) + 2)
                split_low(2, 11)
                hidden_tile(k0, 0, PA_FW, PA_FW + FT * 4)
                split_low(0, 12)
                scale_up(1, 1, uses(l, U_FFN + 1) + 2)
                hidden_low(k0, 0, 0)
                hidden_tile(k0 + 1, 1, PA_FW + 4, PA_FW + FT * 4 + 4)

                def ffn_step(j, parity, last):
                    k = j * 2 + l * FT
                    col = j * 8 + PA_FW
                    scale_up(2, 0, l * USES + j + 12)
                    hidden_low(k - 1, 1, 1 - parity)
                    hidden_tile(k, 0, col, col + FT * 4)
                    split_low(2, j + 11)
                    scale_up(0, 1, l * USES + j + 13)
                    hidden_low(k, 0, parity)
                    hidden_tile(k + 1, 1, col + 4, col + FT * 4 + 4)
                    if not last:
                        split_low(0, j + 12)

                with dve.Fori(0, FFN_STEPS // 2 - 1) as r:
                    ffn_step(r * 2 + 1, 1, False)
                    ffn_step(r * 2 + 2, 0, False)
                ffn_step(FFN_STEPS - 2, 1, False)
                ffn_step(FFN_STEPS - 1, 0, True)
                hidden_low(k0 + FT - 1, 1, 0)
                for i in range(4):
                    if i < 3:
                        dve.wait_ge(down_done, l * 3 + i + 1)
                    else:
                        dve.wait_ge(unit_done[2], l * USES + USES + 1)
                    x2 = x[:, 2 * i:2 * i + 2, :]
                    V.tensor_tensor(x2, down[i][:, :, :], x2, ALU.add).then_inc(x_ready, 1)

            dve.wait_ge(rstd_ready, DEPTH * 3 + 1)
            for t in range(NT):
                V.scalar_tensor_tensor(h32[:, t, :], x[:, t, :], gf[:, t:t + 1], rstd[:, :], ALU.mult, ALU.mult).then_inc(y_ready, 1)

        @block.tensor
        def _(pe):
            MM = nc.tensor.matmul

            def product(out, s, block, hi, lo, start, stop, accumulate=False):
                w = slice(block * P, block * P + P)
                MM(out, whi[s][:, w], hi, start=start, stop=False, skip_group_check=accumulate)
                MM(out, whi[s][:, w], lo, start=False, stop=False, skip_group_check=accumulate)
                return MM(out, wlo[s][:, w], hi, start=False, stop=stop, skip_group_check=accumulate)

            def unit(s, uses_before, hi, lo, ready=None, between=None):
                pe.wait_ge(hi_ready[s], uses_before + 1)
                pe.wait_ge(lo_ready[s], uses_before + 1)
                for m in range(2):
                    if m == 1 and between is not None:
                        between()
                    for k in range(NT):
                        if ready is not None and m == 0 and k % 2 == 0:
                            ready(k // 2)
                        last = product(pu[s][:, m, :], s, 2 * k + m, hi[:, k, :], lo[:, k, :], k == 0, k == NT - 1)
                last.then_inc(unit_done[s], 1)

            def sum_pair(bank, src, p, sem, value):
                pe.wait_ge(sem, value)
                for t in (2 * p, 2 * p + 1):
                    last = MM(bank, ones[:, :], src[:, t, :], start=(t == 0), stop=(t == NT - 1), skip_group_check=True)
                if p == NT // 2 - 1:
                    last.then_inc(stat_done, 1)
                return last

            pe.wait_ge(setup, 2)
            for p in range(NT // 2):
                last = sum_pair(po[:, 0, :], sq, p, sq_ready, p + 1)
                if p < RING:
                    last.then_inc(unit_done[p], 1)
            pe.wait_ge(c_in, 16)
            swap, ident = const[:, C_SWAP:C_SWAP + P], const[:, C_ID:C_ID + P]

            with pe.Fori(0, DEPTH) as l:
                def standard(u, hi, lo, ready=None, between=None):
                    if u >= RING:
                        pe.wait_ge(*result_read(l, u - RING))
                    unit(u % RING, uses(l, u), hi, lo, ready, between)

                def parts_ready(high, high_before, low, low_before):
                    def ready(p):
                        pe.wait_ge(high, high_before + p + 1)
                        pe.wait_ge(low, low_before + p + 1)
                    return ready

                def swap_halves(n, src, tiles):
                    if n:
                        pe.wait_ge(rope_ab, l * 10 + 2 * n)
                    MM(pt[:, 0:tiles, :], swap, src, start=True, stop=True).then_inc(rot_done, 1)

                def scores(n):
                    c, g = n % N_CHUNKS, n // N_CHUNKS
                    keys = slice(max(c - 1, 0) * CHUNK, (c + 1) * CHUNK)
                    pe.wait_ge(rope_done, l * 10 + (6 if g == 0 else 10))
                    if n >= 2:
                        pe.wait_ge(exp_done, l * GROUPS + n - 1)
                    bank = ps[n % 2][:, :, :].rearrange("p a (b t) -> p (a b) t", t=P)
                    for j in range(GROUP_PAIRS):
                        last = MM(bank[:, j, 0:keys.stop - keys.start], qr[:, GROUP_PAIRS * g + j, c, :, :],
                                  kr[:, g, keys], start=True, stop=True)
                    last.then_inc(s_done, 1)

                def transpose_probs(n):
                    pe.wait_ge(p_ready, l * GROUPS + n + 1)
                    pe.wait_ge(rope_ab, l * 10 + 10)
                    if n:
                        pe.wait_ge(pt_ready, l * GROUPS + n)
                    bank = pt[:, :, :].rearrange("p a (b t) -> p (a b) t", t=P)
                    for j in range(GROUP_PAIRS):
                        last = nc.tensor.transpose(bank[:, j, :], probs[n % 2][:, j, :], ident)
                    last.then_inc(tr_done, 1)

                def values(n):
                    c, g = n % N_CHUNKS, n // N_CHUNKS
                    pe.wait_ge(v_ready, l * 2 + 2)
                    pe.wait_ge(pt_ready, l * GROUPS + n + 1)
                    if n:
                        pe.wait_ge(ol_ready, l * GROUPS + n)
                    MM(po[0:HEAD_DIM, :, :], vwin[:, c, HEAD_DIM * g:HEAD_DIM * g + HEAD_DIM], probsT[n % 2][:, :, :],
                       start=True, stop=True).then_inc(pv_done, 1)

                def mean_pair(p):
                    if p == 0:
                        pe.wait_ge(exp_done, l * GROUPS + GROUPS - 1)
                    sum_pair(ps[0][:, 0, :], cv, p, conv_step, (l * (NT // 2) + p + 1) * 2 * TAPS)

                def square_pair(p):
                    sum_pair(ps[1][:, 0, :], sq, p, sq_ready, l * 12 + 4 + p + 1)

                h_ready = parts_ready(hh_ready, l * 8, hl_ready, l * 8)
                for i in range(NT):
                    standard(U_GLU + i, hh, hl, h_ready if i == 0 else None)
                standard(U_KV, hh, hl)
                standard(U_Q, hh, hl)
                pe.wait_ge(kv_raw, l + 1)
                swap_halves(0, kvraw[:, 0:1, :], 1)
                windows = po[:, :, :].rearrange("p a (b t) -> p (a b) t", t=P)
                for c in range(1, N_CHUNKS):
                    nc.tensor.transpose(windows[:, c, :], kvraw[:, 1, CHUNK * (c - 1):CHUNK * (c + 1)], ident)
                nc.tensor.transpose(windows[0:CHUNK, 0, :], kvraw[:, 1, 0:CHUNK], ident).then_inc(vt_done, 1)
                for i in range(4):
                    if i < 3:
                        standard(U_Q + 1 + i, hh, hl)
                    else:
                        scores(0)
                        standard(U_GATE, hh, hl)
                    pe.wait_ge(q_raw, l * 4 + i + 1)
                    swap_halves(1 + i, qraw[i % 2], 2)
                scores(1)
                for i in range(GROUPS):
                    if i + 1 < GROUPS:
                        standard(U_GATE + i + 1, hh, hl)
                    else:
                        mean_pair(0)
                        mean_pair(1)
                    transpose_probs(i)
                    if i:
                        values(i - 1)
                    if i + 2 < GROUPS:
                        scores(i + 2)
                mean_pair(2)
                values(GROUPS - 1)

                def o_ready(p):
                    pe.wait_ge(oh_ready, l * 2 * GROUPS + 2 * GROUPS)
                    pe.wait_ge(ol_ready, l * GROUPS + GROUPS)

                for i in range(2):
                    standard(U_AO + i, oh, ol, o_ready if i == 0 else None)
                mean_pair(3)
                standard(U_AO + 2, oh, ol)
                for p in range(NT // 2):
                    square_pair(p)
                standard(U_AO + 3, oh, ol)
                u_parts = parts_ready(uh_ready, l * 8, ul_ready, l * 8)
                for i in range(4):
                    standard(U_CO + i, uh, ul, u_parts if i == 0 else None)
                merged = parts_ready(hh_ready, l * 8 + 4, hl_ready, l * 8 + 4)
                for i in range(4):
                    standard(U_OUT + i, hh, hl, merged if i == 0 else None)
                    if i >= 1:
                        sum_pair(po[:, 0, :], sq, i - 1, sq_ready, l * 12 + 8 + i)
                scaled = parts_ready(uh_ready, l * 8 + 4, ul_ready, l * 8 + 4)
                standard(U_FFN, uh, ul, scaled, lambda: sum_pair(po[:, 0, :], sq, 3, sq_ready, l * 12 + 12))
                pe.wait_ge(down_zero, l + 1)
                standard(U_FFN + 1, uh, ul)

                def down_unit(s, k, parity):
                    for ab in range(2):
                        pe.wait_ge(fh_ready, k + ab + 1)
                        pe.wait_ge(fl_ready, k + ab + 1)
                        tile = 2 * parity + ab
                        for m in range(NT):
                            last = product(down[m // 2][:, m % 2, :], s, NT * ab + m, fh[:, tile, :], fl[:, tile, :], False, True, True)
                    last.then_inc(unit_done[s], 1)

                def ffn_step(j, parity):
                    k = j * 2 + l * FT
                    n = l * USES + j
                    pe.wait_ge(up_ready, k - 1)
                    unit(2, n + 10, uh, ul)
                    pe.wait_ge(up_ready, k)
                    unit(0, n + 11, uh, ul)
                    pe.wait_ge(hi_ready[1], n + 12)
                    pe.wait_ge(lo_ready[1], n + 12)
                    down_unit(1, k - 2, 1 - parity)

                with pe.Fori(0, FFN_STEPS // 2) as r:
                    ffn_step(r * 2 + 1, 1)
                    ffn_step(r * 2 + 2, 0)
                pe.wait_ge(hi_ready[2], (l + 1) * USES)
                pe.wait_ge(lo_ready[2], (l + 1) * USES)
                pe.wait_ge(fh_ready, (l + 1) * FT)
                pe.wait_ge(fl_ready, (l + 1) * FT)
                for i in range(4):
                    for m in (2 * i, 2 * i + 1):
                        for ab in range(2):
                            last = product(down[i][:, m % 2, :], 2, NT * ab + m, fh[:, ab, :], fl[:, ab, :], False, True, True)
                    if i < 3:
                        last.then_inc(down_done, 1)
                    else:
                        last.then_inc(unit_done[2], 1)
                    if i >= 2:
                        sum_pair(po[:, 0, :], sq, i - 2, sq_ready, l * 12 + 12 + i - 1)
                for p in (2, 3):
                    sum_pair(po[:, 0, :], sq, p, sq_ready, l * 12 + 12 + p + 1)


def kernel(**inputs):
    import numpy as np
    import concourse.bacc as bacc
    from concourse.bass_utils import run_bass_kernel_spmd

    a = {n: np.ascontiguousarray(v) for n, v in inputs.items()}

    def columns(v):
        v = v.reshape(v.shape[:-1] + (v.shape[-1] // P, P))
        return np.moveaxis(v, -1, 0)

    layers = []
    units = np.zeros((DEPTH * UNITS + AHEAD, P, UNIT), np.float32)
    for l in range(DEPTH):
        p = np.empty((P, NPAR), np.float32)
        for at, name in ((PA_G, "attn_norm_g"), (PA_CB, "conv_dw_b"), (PA_LG, "conv_ln_g"), (PA_LB, "conv_ln_b"), (PA_FG, "ffn_norm_g")):
            p[:, at:at + NT] = columns(a[name][l])
        p[:, PA_CW:PA_SINK] = columns(a["conv_dw_w"][l]).transpose(0, 2, 1).reshape(P, -1)
        p[:, PA_SINK:PA_FW] = np.repeat(a["attn_sinks"][l].reshape(N_PAIRS, 2).T, HEAD_DIM, axis=0)
        taps = columns(np.concatenate([a["ffn_dw_w"][l], a["ffn_dw_b"][l][None]]))
        p[:, PA_FW:] = taps.transpose(0, 2, 1).reshape(P, -1)
        layers.append(p)

        w_in = a["w_in"][l].reshape(NT, P, -1, P)
        kv, q, glu, gates = 8, 0, 10, 26
        order = [(w_in, glu + i, glu + NT + i) for i in range(NT)] + [(w_in, kv, kv + 1)]
        order += [(w_in, q + 2 * i, q + 2 * i + 1) for i in range(4)]
        order += [(w_in, gates + i, gates + NT + i) for i in range(NT)]
        for name in ("w_attn_o", "w_conv_o", "w_out"):
            w = a[name][l].reshape(NT, P, -1, P)
            order += [(w, 2 * i, 2 * i + 1) for i in range(4)]
        up = a["w_ffn_up"][l].reshape(NT, P, -1, P)
        ups = [(up, i, FT + i) for i in range(FT)]
        down = a["w_ffn_down"][l].reshape(FFN_STEPS, 2, P, D_MODEL)
        order += ups[0:2]
        for j in range(1, FFN_STEPS):
            order += [ups[2 * j], ups[2 * j + 1], down[j - 1]]
        order += [down[FFN_STEPS - 1]]
        for n, item in enumerate(order):
            if isinstance(item, tuple):
                w, c0, c1 = item
                block = w[:, :, [c0, c1], :].transpose(1, 0, 2, 3)
            else:
                block = item.transpose(1, 0, 2)
            units[l * UNITS + n] = block.reshape(P, UNIT)

    const = np.zeros((P, NCONST), np.float32)
    d = np.arange(P)
    const[:, C_FREQ] = THETA ** (-(d % 32) / 32.0)
    const[d ^ 32, C_SWAP + d] = np.where(d % 64 < 32, -1.0, 1.0)
    const[d, C_ID + d] = 1.0
    const[:, C_EPS], const[:, C_HALFPI] = EPS, np.pi / 2

    arrays = {
        "x_t": np.ascontiguousarray(columns(a["x"][0]).transpose(0, 2, 1)),
        "positions": a["positions"].reshape(1, SEQ) if a["positions"].dtype == np.int32 else a["positions"],
        "const": const,
        "params": np.ascontiguousarray(np.concatenate(layers, axis=1)),
        "final_g": np.ascontiguousarray(columns(a["final_norm_g"])),
        "weights": units,
    }
    nc = bacc.Bacc("TRN2", target_bir_lowering=False, num_devices=1)
    args = [nc.dram_tensor("in_" + n, v.shape, mybir.dt.from_np(v.dtype), kind="ExternalInput").ap() for n, v in arrays.items()]
    out = nc.dram_tensor("out_y", (P, NT, SEQ), mybir.dt.float32, kind="ExternalOutput").ap()
    hybrid_encoder(nc, *args, out)
    r = run_bass_kernel_spmd(nc, [{"in_" + n: v for n, v in arrays.items()}], core_ids=[0])
    y = r.results[0]["out_y"]
    return np.ascontiguousarray(y.transpose(2, 1, 0)).reshape(1, SEQ, D_MODEL)
```
